# Optimizing a Trainium2 kernel written in Bass

```python
import math
import jax, jax.numpy as jnp
from jax import lax
import numpy as np

D_MODEL = 1024
BATCH = 1
SEQ = 1024
DEPTH = 1
DEC_BATCH = 8
DEC_SEQ = 4
PAST_LEN = 2048
PAGE_SIZE = 128

DH = 64
NSA_H = 8
NSA_KVH = 2
NSA_R = NSA_H // NSA_KVH
CMP_L = 32
CMP_S = 16
CMP_HID = 128
SEL_L = 64
SEL_N = 16
WIN = 512
SSD_H = 8
SSD_P = 64
SSD_INNER = SSD_H * SSD_P
SSD_G = 2
SSD_N = 64
SSD_CONV = 4
SSD_CONV_DIM = SSD_INNER + 2 * SSD_G * SSD_N
SSD_CHUNK = 128
DIL_PAIRS = ((128, 1), (512, 4), (2048, 16))
DIL_HG = 4
DIL_H = DIL_HG * len(DIL_PAIRS)
MEM_LEN = 256
MEM_H = 4
MEM_DH = 64
D_FF = 2816
FFN_CONV = 3

Q_BLOCK = 128
EPS = 1e-6
NEG = -1.0e30
FORCE_BONUS = 1.0e4
IN_SIZES = (NSA_H * DH, 6 * NSA_KVH * DH, 3 * NSA_H, SSD_INNER, SSD_CONV_DIM, SSD_H, 3 * DIL_H * DH, 3 * D_MODEL)
IN_COLS = sum(IN_SIZES)

kernel_name = 'hybrid_nsa_ssd_dilated_decoder_step'

def rms_norm(x, g):
    xf = x.astype(jnp.float32)
    y = xf * lax.rsqrt(jnp.mean(xf * xf, axis=-1, keepdims=True) + EPS)
    return (y * g.astype(jnp.float32)).astype(x.dtype)

def alibi_slopes(n):
    return jnp.asarray([2.0 ** (-8.0 * (i + 1) / n) for i in range(n)], jnp.float32)

def split_in(proj):
    out, o = [], 0
    for s in IN_SIZES:
        out.append(proj[..., o:o + s])
        o += s
    return out

def last_rows(a, n):
    if a.shape[1] < n:
        a = jnp.pad(a, [(0, 0), (n - a.shape[1], 0)] + [(0, 0)] * (a.ndim - 2))
    return a[:, a.shape[1] - n:]

def attn_probs(q, k, dist, valid, slopes):
    s = jnp.einsum('bnqgrd,bnkgd->bngrqk', q, k, preferred_element_type=jnp.float32) * (q.shape[-1] ** -0.5)
    s = s - slopes[None, None, :, :, None, None] * dist[:, :, None, None].astype(jnp.float32)
    s = jnp.where(valid[:, :, None, None], s, NEG)
    m = jnp.max(s, axis=-1, keepdims=True)
    e = jnp.exp(s - m)
    den = jnp.sum(e, axis=-1, keepdims=True)
    return e / den, (m + jnp.log(den))[..., 0]

def attn_core(q, k, v, dist, valid, slopes):
    p, lse = attn_probs(q, k, dist, valid, slopes)
    o = jnp.einsum('bngrqk,bnkgd->bnqgrd', p.astype(v.dtype), v)
    return o, lse

def banded_attn(q, k, v, slopes, max_dist):
    B, L, G, R, dh = q.shape
    blk = min(Q_BLOCK, L)
    nb = -(-L // blk)
    pad_end = nb * blk - L
    span = max_dist
    qp = jnp.pad(q, ((0, 0), (0, pad_end), (0, 0), (0, 0), (0, 0)))
    kp = jnp.pad(k, ((0, 0), (span, pad_end), (0, 0), (0, 0)))
    vp = jnp.pad(v, ((0, 0), (span, pad_end), (0, 0), (0, 0)))
    kidx = jnp.arange(nb)[:, None] * blk + jnp.arange(span + blk)[None]
    qb = jnp.moveaxis(qp.reshape(B, nb, blk, G, R, dh), 1, 0)
    kb = jnp.moveaxis(kp[:, kidx], 1, 0)
    vb = jnp.moveaxis(vp[:, kidx], 1, 0)
    qpos = jnp.arange(nb * blk).reshape(nb, blk)
    kpos = kidx - span
    dist = qpos[:, :, None] - kpos[:, None, :]
    valid = (dist >= 0) & (dist <= max_dist) & (kpos[:, None, :] >= 0)

    def one(args):
        qi, ki, vi, di, mi = args
        return attn_core(qi[:, None], ki[:, None], vi[:, None], di[None, None], mi[None, None], slopes)

    o, lse = lax.map(one, (qb, kb, vb, dist, valid))
    o = jnp.moveaxis(o[:, :, 0], 0, 1).reshape(B, nb * blk, G, R, dh)[:, :L]
    lse = jnp.transpose(lse[:, :, 0], (1, 0, 4, 2, 3)).reshape(B, nb * blk, G, R)[:, :L]
    return o, lse

def nsa_compress(kr, pe, w1, w2):
    B, L, G, dh = kr.shape
    n = (L - CMP_L) // CMP_S + 1
    r = CMP_L // CMP_S
    chunks = kr[:, :(n + r - 1) * CMP_S].reshape(B, n + r - 1, CMP_S, G, dh)
    blocks = jnp.concatenate([chunks[:, j:j + n] for j in range(r)], axis=2) + pe[None, None, :, None]
    flat = jnp.swapaxes(blocks, 2, 3).reshape(B, n, G, CMP_L * dh)
    return jax.nn.silu(flat @ w1) @ w2

def nsa_cmp_sel(q, qpos, kc, vc, ksb, vsb, slopes):
    B, Q, G, R, dh = q.shape
    n_cmp = kc.shape[1]
    n_sel = ksb.shape[2]
    c_end = jnp.arange(n_cmp) * CMP_S + (CMP_L - 1)
    dist_c = qpos[:, None] - c_end[None]
    valid_c = dist_c >= 0
    p_c, _ = attn_probs(q[:, None], kc[:, None], dist_c[None, None], valid_c[None, None], slopes)
    p_c = jnp.where(valid_c, p_c[:, 0], 0.0)
    o_c = jnp.einsum('bgrqn,bngd->bqgrd', p_c.astype(vc.dtype), vc)
    imp = p_c.sum(axis=2)
    ratio = SEL_L // CMP_S
    front = CMP_L // CMP_S - 1
    n_ov = ratio + front
    imp = jnp.pad(imp, ((0, 0), (0, 0), (0, 0), (front, ratio * n_sel + n_ov - front - n_cmp)))
    imp_sel = sum(imp[..., o:o + ratio * n_sel:ratio] for o in range(n_ov))
    j = jnp.arange(n_sel)
    cur = (qpos // SEL_L)[:, None]
    forced = (j[None] == 0) | (j[None] == cur) | (j[None] == cur - 1)
    causal = j[None] * SEL_L <= qpos[:, None]
    score = jnp.where(causal, imp_sel + jnp.where(forced, FORCE_BONUS, 0.0), NEG)
    k_top = min(SEL_N, n_sel)
    top_v, top_i = lax.top_k(score, k_top)
    blk_ok = top_v > 0.5 * NEG
    gather = jax.vmap(jax.vmap(lambda a, i: a[i]))
    kg = gather(ksb, top_i)
    vg = gather(vsb, top_i)
    kpos = top_i[..., None] * SEL_L + jnp.arange(SEL_L)
    dist_s = qpos[:, None, None] - kpos
    valid_s = blk_ok[..., None] & (dist_s >= 0)
    s = jnp.einsum('bqgrd,bgqkld->bgrqkl', q, kg, preferred_element_type=jnp.float32) * (dh ** -0.5)
    s = s - slopes[None, :, :, None, None, None] * dist_s[:, :, None].astype(jnp.float32)
    s = jnp.where(valid_s[:, :, None], s, NEG).reshape(B, G, R, Q, k_top * SEL_L)
    e = jnp.exp(s - jnp.max(s, axis=-1, keepdims=True))
    p_s = e / jnp.sum(e, axis=-1, keepdims=True)
    o_s = jnp.einsum('bgrqm,bgqmd->bqgrd', p_s.astype(vg.dtype), vg.reshape(B, G, Q, k_top * SEL_L, dh))
    return o_c, o_s

def nsa_global(q, qpos, glob, pe, w1, w2, slopes):
    B, T, G, R, dh = q.shape
    L = glob.shape[1]
    kc = nsa_compress(glob[:, :, 0], pe[0], w1[0], w2[0])
    vc = nsa_compress(glob[:, :, 1], pe[1], w1[1], w2[1])
    n_sel = -(-L // SEL_L)

    def to_blocks(a):
        a = jnp.pad(a, ((0, 0), (0, n_sel * SEL_L - L), (0, 0), (0, 0)))
        return a.reshape(B, n_sel, SEL_L, G, dh).transpose(0, 3, 1, 2, 4)

    ksb, vsb = to_blocks(glob[:, :, 2]), to_blocks(glob[:, :, 3])
    blk = min(Q_BLOCK, T)
    nb = T // blk
    qb = jnp.moveaxis(q.reshape(B, nb, blk, G, R, dh), 1, 0)
    pb = qpos.reshape(nb, blk)
    o_c, o_s = lax.map(lambda a: nsa_cmp_sel(a[0], a[1], kc, vc, ksb, vsb, slopes), (qb, pb))
    return (jnp.moveaxis(o_c, 0, 1).reshape(B, T, G, R, dh), jnp.moveaxis(o_s, 0, 1).reshape(B, T, G, R, dh))

def ssd_scan(x, dt, A, Bm, Cm, h0):
    f32 = jnp.float32
    B_, T, H, P = x.shape
    rep = H // Bm.shape[2]
    Q = min(SSD_CHUNK, T)
    nc = T // Q
    xc = x.astype(f32).reshape(B_, nc, Q, H, P)
    Bc = jnp.repeat(Bm.astype(f32), rep, axis=2).reshape(B_, nc, Q, H, -1)
    Cc = jnp.repeat(Cm.astype(f32), rep, axis=2).reshape(B_, nc, Q, H, -1)
    dtc = dt.reshape(B_, nc, Q, H)
    acum = jnp.cumsum(dtc * A, axis=2)
    seg = acum[:, :, :, None, :] - acum[:, :, None, :, :]
    tril = jnp.tril(jnp.ones((Q, Q), bool))
    decay = jnp.exp(jnp.where(tril[None, None, :, :, None], seg, NEG))
    cb = jnp.einsum('bcihn,bcjhn->bcijh', Cc, Bc) * decay * dtc[:, :, None]
    y_diag = jnp.einsum('bcijh,bcjhp->bcihp', cb, xc)
    w_end = jnp.exp(acum[:, :, -1:] - acum) * dtc
    states = jnp.einsum('bcjhn,bcjh,bcjhp->bchpn', Bc, w_end, xc)
    chunk_decay = jnp.exp(acum[:, :, -1])

    def step(h, inp):
        s_c, dec = inp
        return h * dec[:, :, None, None] + s_c, h

    h_last, h_in = lax.scan(step, h0.astype(f32), (jnp.moveaxis(states, 1, 0), jnp.moveaxis(chunk_decay, 1, 0)))
    h_in = jnp.moveaxis(h_in, 0, 1)
    y_off = jnp.einsum('bcihn,bchpn,bcih->bcihp', Cc, h_in, jnp.exp(acum))
    return (y_diag + y_off).reshape(B_, T, H, P), h_last

def ssd_mixer(z, xbc, dt_raw, conv0, h0, lp):
    B, T, _ = xbc.shape
    xpad = jnp.concatenate([conv0, xbc], axis=1)
    cw = lp['ssd_conv_w']
    conv = lp['ssd_conv_b'] + sum(xpad[:, k:k + T] * cw[k] for k in range(SSD_CONV))
    xbc_c = jax.nn.silu(conv)
    xs = xbc_c[..., :SSD_INNER].reshape(B, T, SSD_H, SSD_P)
    Bm = xbc_c[..., SSD_INNER:SSD_INNER + SSD_G * SSD_N].reshape(B, T, SSD_G, SSD_N)
    Cm = xbc_c[..., SSD_INNER + SSD_G * SSD_N:].reshape(B, T, SSD_G, SSD_N)
    dt = jax.nn.softplus(dt_raw.astype(jnp.float32) + lp['ssd_dt_bias'].astype(jnp.float32))
    A = -jnp.exp(lp['ssd_a_log'].astype(jnp.float32))
    y, h = ssd_scan(xs, dt, A, Bm, Cm, h0)
    y = y.astype(xs.dtype) + lp['ssd_d'][:, None] * xs
    y = rms_norm(y.reshape(B, T, SSD_INNER) * jax.nn.silu(z), lp['ssd_norm_g'])
    return y, xpad[:, -(SSD_CONV - 1):], h.astype(xbc.dtype)

def dilated_prompt(qkv, slopes):
    B, T = qkv.shape[:2]
    outs, lses, bufs = [], [], []
    for gi, (w, d) in enumerate(DIL_PAIRS):
        sl = slice(gi * DIL_HG, (gi + 1) * DIL_HG)

        def fold(a):
            a = a.reshape(B, T // d, d, DIL_HG, DH)
            return jnp.swapaxes(a, 1, 2).reshape(B * d, T // d, DIL_HG, DH)

        qf, kf, vf = fold(qkv[:, :, 0, sl]), fold(qkv[:, :, 1, sl]), fold(qkv[:, :, 2, sl])
        o, lse = banded_attn(qf[:, :, :, None], kf, vf, (slopes[sl] * d)[:, None], w // d)
        o = jnp.swapaxes(o[:, :, :, 0].reshape(B, d, T // d, DIL_HG, DH), 1, 2).reshape(B, T, DIL_HG, DH)
        lse = jnp.swapaxes(lse[..., 0].reshape(B, d, T // d, DIL_HG), 1, 2).reshape(B, T, DIL_HG)
        outs.append(o)
        lses.append(lse)
        bufs.append(last_rows(qkv[:, :, 1:, sl], min(w, PAST_LEN)))
    return outs, lses, bufs

def dilated_sample(qkv, old_bufs, slopes):
    B, T = qkv.shape[:2]
    outs, lses, bufs = [], [], []
    for gi, (w, d) in enumerate(DIL_PAIRS):
        sl = slice(gi * DIL_HG, (gi + 1) * DIL_HG)
        kv = jnp.concatenate([old_bufs[gi], qkv[:, :, 1:, sl]], axis=1)
        wb = old_bufs[gi].shape[1]
        nk = w // d + 1
        off = d * jnp.arange(nk)
        idx = wb + jnp.arange(T)[:, None] - off[None]
        valid = idx >= 0
        kg = kv[:, jnp.maximum(idx, 0)]
        dist = jnp.broadcast_to(off[None], (T, nk))
        o, lse = attn_core(qkv[:, :, 0, sl][:, :, None, :, None], kg[:, :, :, 0], kg[:, :, :, 1],
                           dist[None, :, None], valid[None, :, None], slopes[sl][:, None])
        outs.append(o[:, :, 0, :, 0])
        lses.append(lse[..., 0, 0])
        bufs.append(kv[:, kv.shape[1] - wb:])
    return outs, lses, bufs

def combine_groups(outs, lses):
    a = jax.nn.softmax(jnp.stack(lses, axis=-1), axis=-1).astype(outs[0].dtype)
    o = jnp.einsum('bthgd,bthg->bthd', jnp.stack(outs, axis=3), a)
    return o.reshape(o.shape[0], o.shape[1], DIL_HG * DH)

def cross_attn(u, mkv, w_mq, w_mo):
    B, T, _ = u.shape
    q = (u @ w_mq).reshape(B, T, MEM_H, MEM_DH)
    s = jnp.einsum('bthd,bmhd->bhtm', q, mkv[:, :, 0], preferred_element_type=jnp.float32) * (MEM_DH ** -0.5)
    p = jax.nn.softmax(s, axis=-1).astype(u.dtype)
    o = jnp.einsum('bhtm,bmhd->bthd', p, mkv[:, :, 1])
    return o.reshape(B, T, MEM_H * MEM_DH) @ w_mo

def conv_ffn(u, conv0, lp):
    T = u.shape[1]
    h = u @ lp['ffn_w_up']
    hp = jnp.concatenate([conv0, h], axis=1)
    cw = lp['ffn_conv_w']
    c = lp['ffn_conv_b'] + sum(hp[:, k:k + T] * cw[k] for k in range(FFN_CONV))
    y = (jax.nn.silu(c[..., :D_FF]) * c[..., D_FF:]) @ lp['ffn_w_down']
    return y, hp[:, -(FFN_CONV - 1):]

def trunk_layer(x, mem_kv, lp, st, past_len):
    B, T, _ = x.shape
    prompt = st is None
    new = {}
    pos = past_len + jnp.arange(T)
    u = rms_norm(x, lp['norm_g'][0])
    nq, nkv, ngate, sz, sxbc, sdt, dqkv, mg = split_in(u @ lp['w_in'])

    slopes_a = alibi_slopes(NSA_H).reshape(NSA_KVH, NSA_R)
    q_a = nq.reshape(B, T, NSA_KVH, NSA_R, DH)
    kv_a = nkv.reshape(B, T, 6, NSA_KVH, DH)
    new['nsa_kv'] = kv_a[:, :, :4]
    if prompt:
        glob = kv_a[:, :, :4]
        o_w = banded_attn(q_a, kv_a[:, :, 4], kv_a[:, :, 5], slopes_a, WIN - 1)[0]
        new['nsa_win'] = last_rows(kv_a[:, :, 4:], min(WIN, PAST_LEN))
    else:
        glob = jnp.concatenate([st['nsa_pages'].reshape(B, past_len, 4, NSA_KVH, DH), kv_a[:, :, :4]], axis=1)
        wb = st['nsa_win'].shape[1]
        buf = jnp.concatenate([st['nsa_win'], kv_a[:, :, 4:]], axis=1)
        kpos = past_len - wb + jnp.arange(wb + T)
        dist = pos[:, None] - kpos[None]
        valid = (dist >= 0) & (dist < WIN) & (kpos[None] >= 0)
        o_w = attn_core(q_a[:, None], buf[:, None, :, 0], buf[:, None, :, 1], dist[None, None], valid[None, None], slopes_a)[0][:, 0]
        new['nsa_win'] = buf[:, buf.shape[1] - wb:]
    o_c, o_s = nsa_global(q_a, pos, glob, lp['nsa_pe'], lp['nsa_cmp_w1'], lp['nsa_cmp_w2'], slopes_a)
    g_a = jax.nn.sigmoid(ngate.reshape(B, T, NSA_KVH, NSA_R, 3).astype(jnp.float32)).astype(x.dtype)
    o_a = (g_a[..., 0:1] * o_c + g_a[..., 1:2] * o_s + g_a[..., 2:3] * o_w).reshape(B, T, NSA_H * DH) @ lp['w_br_a']

    conv0 = jnp.zeros((B, SSD_CONV - 1, SSD_CONV_DIM), x.dtype) if prompt else st['ssd_conv']
    h0 = jnp.zeros((B, SSD_H, SSD_P, SSD_N), x.dtype) if prompt else st['ssm']
    y_b, new['ssd_conv'], new['ssm'] = ssd_mixer(sz, sxbc, sdt, conv0, h0, lp)
    o_b = y_b @ lp['w_br_b']

    slopes_c = alibi_slopes(DIL_H)
    qkv = dqkv.reshape(B, T, 3, DIL_H, DH)
    if prompt:
        outs, lses, new['dil'] = dilated_prompt(qkv, slopes_c)
    else:
        outs, lses, new['dil'] = dilated_sample(qkv, st['dil'], slopes_c)
    o_cc = combine_groups(outs, lses) @ lp['w_br_c']

    gates = jax.nn.sigmoid(mg.reshape(B, T, 3, D_MODEL).astype(jnp.float32)).astype(x.dtype)
    mix = (gates[:, :, 0] * o_a + gates[:, :, 1] * o_b + gates[:, :, 2] * o_cc) @ lp['w_out']
    x = x + rms_norm(mix, lp['norm_g'][1])

    u = rms_norm(x, lp['norm_g'][2])
    x = x + rms_norm(cross_attn(u, mem_kv, lp['w_mq'], lp['w_mo']), lp['norm_g'][3])

    u = rms_norm(x, lp['norm_g'][4])
    fc0 = jnp.zeros((B, FFN_CONV - 1, 2 * D_FF), x.dtype) if prompt else st['ffn_conv']
    f, new['ffn_conv'] = conv_ffn(u, fc0, lp)
    x = x + rms_norm(f, lp['norm_g'][5])
    return x, new

def setup_inputs(seed: int = 0) -> dict:
    key = jax.random.key(seed)
    ks = iter(jax.random.split(key, 48))

    def nrm(shape, scale):
        return jax.random.normal(next(ks), shape, jnp.float32) * scale

    n_pages = PAST_LEN // PAGE_SIZE
    n_used = DEC_BATCH * n_pages
    n_phys = n_used + max(1, n_used // 4)
    page_table = jax.random.permutation(next(ks), n_phys)[:n_used].reshape(DEC_BATCH, n_pages).astype(jnp.int32)
    dt0 = jnp.exp(jax.random.uniform(next(ks), (DEPTH, SSD_H), jnp.float32, math.log(1e-3), math.log(1e-1)))
    return {
        'x_prompt': nrm((BATCH, SEQ, D_MODEL), 1.0),
        'x_sample': nrm((DEC_BATCH, DEC_SEQ, D_MODEL), 1.0),
        'cache_nsa_kv': nrm((DEPTH, n_phys, PAGE_SIZE, 4, NSA_KVH, DH), 1.0),
        'cache_nsa_win': nrm((DEPTH, DEC_BATCH, min(WIN, PAST_LEN), 2, NSA_KVH, DH), 1.0),
        'state_ssm': nrm((DEPTH, DEC_BATCH, SSD_H, SSD_P, SSD_N), 0.3),
        'state_ssd_conv': nrm((DEPTH, DEC_BATCH, SSD_CONV - 1, SSD_CONV_DIM), 1.0),
        'cache_dil_w128': nrm((DEPTH, DEC_BATCH, min(DIL_PAIRS[0][0], PAST_LEN), 2, DIL_HG, DH), 1.0),
        'cache_dil_w512': nrm((DEPTH, DEC_BATCH, min(DIL_PAIRS[1][0], PAST_LEN), 2, DIL_HG, DH), 1.0),
        'cache_dil_w2048': nrm((DEPTH, DEC_BATCH, min(DIL_PAIRS[2][0], PAST_LEN), 2, DIL_HG, DH), 1.0),
        'cache_mem_kv': nrm((DEPTH, DEC_BATCH, MEM_LEN, 2, MEM_H, MEM_DH), 1.0),
        'state_ffn_conv': nrm((DEPTH, DEC_BATCH, FFN_CONV - 1, 2 * D_FF), 1.0),
        'page_table': page_table,
        'mem_prompt': nrm((BATCH, MEM_LEN, D_MODEL), 1.0),
        'norm_g': 1.0 + nrm((DEPTH, 6, D_MODEL), 0.05),
        'w_in': nrm((DEPTH, D_MODEL, IN_COLS), D_MODEL ** -0.5),
        'nsa_pe': nrm((DEPTH, 2, CMP_L, DH), 0.1),
        'nsa_cmp_w1': nrm((DEPTH, 2, CMP_L * DH, CMP_HID), (CMP_L * DH) ** -0.5),
        'nsa_cmp_w2': nrm((DEPTH, 2, CMP_HID, DH), CMP_HID ** -0.5),
        'ssd_conv_w': nrm((DEPTH, SSD_CONV, SSD_CONV_DIM), SSD_CONV ** -0.5),
        'ssd_conv_b': nrm((DEPTH, SSD_CONV_DIM), 0.02),
        'ssd_dt_bias': dt0 + jnp.log(-jnp.expm1(-dt0)),
        'ssd_a_log': jnp.log(jax.random.uniform(next(ks), (DEPTH, SSD_H), jnp.float32, 1.0, 16.0)),
        'ssd_d': 1.0 + nrm((DEPTH, SSD_H), 0.1),
        'ssd_norm_g': 1.0 + nrm((DEPTH, SSD_INNER), 0.05),
        'w_br_a': nrm((DEPTH, NSA_H * DH, D_MODEL), (NSA_H * DH) ** -0.5),
        'w_br_b': nrm((DEPTH, SSD_INNER, D_MODEL), SSD_INNER ** -0.5),
        'w_br_c': nrm((DEPTH, DIL_HG * DH, D_MODEL), (DIL_HG * DH) ** -0.5),
        'w_out': nrm((DEPTH, D_MODEL, D_MODEL), D_MODEL ** -0.5),
        'mem_norm_g': 1.0 + nrm((DEPTH, D_MODEL), 0.05),
        'w_mq': nrm((DEPTH, D_MODEL, MEM_H * MEM_DH), D_MODEL ** -0.5),
        'w_mkv': nrm((DEPTH, D_MODEL, 2 * MEM_H * MEM_DH), D_MODEL ** -0.5),
        'w_mo': nrm((DEPTH, MEM_H * MEM_DH, D_MODEL), (MEM_H * MEM_DH) ** -0.5),
        'ffn_w_up': nrm((DEPTH, D_MODEL, 2 * D_FF), D_MODEL ** -0.5),
        'ffn_conv_w': nrm((DEPTH, FFN_CONV, 2 * D_FF), FFN_CONV ** -0.5),
        'ffn_conv_b': nrm((DEPTH, 2 * D_FF), 0.02),
        'ffn_w_down': nrm((DEPTH, D_FF, D_MODEL), D_FF ** -0.5),
    }

def reference(x_prompt, x_sample, cache_nsa_kv, cache_nsa_win, state_ssm, state_ssd_conv,
              cache_dil_w128, cache_dil_w512, cache_dil_w2048, cache_mem_kv, state_ffn_conv,
              page_table, mem_prompt, norm_g, w_in, nsa_pe, nsa_cmp_w1, nsa_cmp_w2,
              ssd_conv_w, ssd_conv_b, ssd_dt_bias, ssd_a_log, ssd_d, ssd_norm_g,
              w_br_a, w_br_b, w_br_c, w_out, mem_norm_g, w_mq, w_mkv, w_mo,
              ffn_w_up, ffn_conv_w, ffn_conv_b, ffn_w_down):
    past_len = page_table.shape[1] * cache_nsa_kv.shape[2]
    xp, xs = x_prompt, x_sample
    new_p, new_s, mem_new = [], [], []
    for l in range(DEPTH):
        lp = {'norm_g': norm_g[l], 'w_in': w_in[l], 'nsa_pe': nsa_pe[l], 'nsa_cmp_w1': nsa_cmp_w1[l],
              'nsa_cmp_w2': nsa_cmp_w2[l], 'ssd_conv_w': ssd_conv_w[l], 'ssd_conv_b': ssd_conv_b[l],
              'ssd_dt_bias': ssd_dt_bias[l], 'ssd_a_log': ssd_a_log[l], 'ssd_d': ssd_d[l],
              'ssd_norm_g': ssd_norm_g[l], 'w_br_a': w_br_a[l], 'w_br_b': w_br_b[l], 'w_br_c': w_br_c[l],
              'w_out': w_out[l], 'w_mq': w_mq[l], 'w_mo': w_mo[l], 'ffn_w_up': ffn_w_up[l],
              'ffn_conv_w': ffn_conv_w[l], 'ffn_conv_b': ffn_conv_b[l], 'ffn_w_down': ffn_w_down[l]}
        mkv = (rms_norm(mem_prompt, mem_norm_g[l]) @ w_mkv[l]).reshape(mem_prompt.shape[0], MEM_LEN, 2, MEM_H, MEM_DH)
        mem_new.append(mkv)
        xp, sp = trunk_layer(xp, mkv, lp, None, 0)
        st = {'nsa_pages': cache_nsa_kv[l, page_table], 'nsa_win': cache_nsa_win[l], 'ssm': state_ssm[l],
              'ssd_conv': state_ssd_conv[l], 'dil': (cache_dil_w128[l], cache_dil_w512[l], cache_dil_w2048[l]),
              'ffn_conv': state_ffn_conv[l]}
        xs, ss = trunk_layer(xs, cache_mem_kv[l], lp, st, past_len)
        new_p.append(sp)
        new_s.append(ss)

    def stk(lst, name):
        return jnp.stack([d[name] for d in lst])

    def stk_dil(lst, g):
        return jnp.stack([d['dil'][g] for d in lst])

    y_prompt, y_sample = xp, xs
    return (y_prompt, y_sample,
            stk(new_p, 'nsa_kv'), stk(new_s, 'nsa_kv'),
            stk(new_p, 'nsa_win'), stk(new_s, 'nsa_win'),
            stk(new_p, 'ssm'), stk(new_s, 'ssm'),
            stk(new_p, 'ssd_conv'), stk(new_s, 'ssd_conv'),
            stk_dil(new_p, 0), stk_dil(new_s, 0),
            stk_dil(new_p, 1), stk_dil(new_s, 1),
            stk_dil(new_p, 2), stk_dil(new_s, 2),
            jnp.stack(mem_new),
            stk(new_p, 'ffn_conv'), stk(new_s, 'ffn_conv'))


_drawn_inputs = setup_inputs


def setup_inputs(seed=0):
    import zlib

    import numpy as np

    out = dict(_drawn_inputs(seed))
    spreads = {}
    factors = {'nsa_pe': 2.874, 'ffn_conv_b': 3.966}
    for name, (base, spread) in spreads.items():
        noise = np.random.default_rng([zlib.crc32(name.encode()), seed]).standard_normal(out[name].shape)
        drawn = base * np.exp(spread * noise) if base else spread * noise
        out[name] = __import__('jax').numpy.asarray(drawn.astype(out[name].dtype))
    for name, factor in factors.items():
        out[name] = (out[name] * factor).astype(out[name].dtype)
    return out
```

```python
from contextlib import ExitStack

import numpy as np

import concourse.bass as bass
from concourse import mybir

F32 = mybir.dt.float32
I32 = mybir.dt.int32
ALU = mybir.AluOpType
ACT = mybir.ActivationFunctionType
AX = mybir.AxisListType

P = 128
D = 1024
DK = D // P
SEQ = 1024
PT = SEQ // P
DB, DT = 8, 4
NS = DB * DT
TOK = SEQ + NS
TILES = [(t * P, P) for t in range(PT)] + [(SEQ, NS)]
PAST = 2048
PAGE = 128
NPAGES = PAST // PAGE
DH = 64
NSA_H, KVH, NSA_R = 8, 2, 4
CMP_L, CMP_S, HID = 32, 16, 128
SEL_L, SEL_N = 64, 16
WIN = 512
SH, SP, SG, SN = 8, 64, 2, 64
SIN = SH * SP
SCONV = 4
SCD = SIN + 2 * SG * SN
DIL = ((128, 1), (512, 4), (2048, 16))
DG = 4
DILH = DG * len(DIL)
MEM = 256
DFF = 2816
FFK = DFF // P
EPS = 1e-6
BIG = 1.0e30
FORCE = 1.0e4
NCMP = (PAST + DT - CMP_L) // CMP_S + 1
NCMP_P = (SEQ - CMP_L) // CMP_S + 1
NSEL = -(-(PAST + DT) // SEL_L)

C_Q = 0
C_KV = C_Q + NSA_H * DH
C_GATE = C_KV + 6 * KVH * DH
C_Z = C_GATE + 3 * NSA_H
C_XBC = C_Z + SIN
C_DT = C_XBC + SCD
C_DIL = C_DT + SH
C_MG = C_DIL + 3 * DILH * DH
COLS = C_MG + 3 * D
O_A, O_B, O_C = 0, NSA_H * DH, NSA_H * DH + SIN
O_COLS = O_C + DG * DH
OK = O_COLS // P
DCOL = 2 * DH + 4


class Stage:

    def __init__(self, nc, name):
        self.nc, self.name, self.stack, self.sems = nc, name, ExitStack(), []

    def __enter__(self):
        return self

    def __exit__(self, *exc):
        self.stack.close()
        if self.sems and exc[0] is None:
            with self.nc.Block() as block:
                @block.gpsimd
                def _(pool):
                    for sem in self.sems:
                        pool.sem_clear(sem)
            for sem in self.sems:
                self.nc.release_semaphore(sem)

    def sb(self, name, shape, dt=F32):
        return self.stack.enter_context(self.nc.sbuf_tensor(f"{self.name}_{name}", shape, dt))

    def ps(self, name, shape):
        return self.stack.enter_context(self.nc.psum_tensor(f"{self.name}_{name}", shape, F32))

    def sem(self, name):
        self.sems.append(self.nc.alloc_semaphore(f"{self.name}_{name}"))
        return self.sems[-1]


def stand(eng, aside):
    eng.sem_inc(aside, 1)


def wide(ap, n):
    return ap.unsqueeze(2).broadcast_to([ap.shape[0], ap.shape[1], n])


def norm_transposed(nc, name, tiles, rows_of, gain, ident, out_T):
    with Stage(nc, name) as st:
        xt = st.sb("x", [P, 2, D])
        junk = st.sb("junk", [P, D])
        ss = st.sb("ss", [P, 4, 2])
        grow = st.sb("grow", [DK, P])
        gcol = st.sb("gcol", [P, DK])
        ps = [st.ps(f"ps{i}", [P, 4, P]) for i in range(4)]
        gain_in, x_in = st.sem("gain_in"), [st.sem("x_in0"), st.sem("x_in1")]
        squared, meaned, rooted, scaled = st.sem("squared"), st.sem("meaned"), st.sem("rooted"), st.sem("scaled")
        turned, copied = st.sem("turned"), st.sem("copied")
        gain_turned, gain_ready = st.sem("gain_turned"), st.sem("gain_ready")
        n = len(tiles)
        with nc.Block() as block:
            @block.sync
            def _(sp):
                sp.dma_start(grow[:, :], gain).then_inc(gain_in, 16)
                for t, (r0, m) in enumerate(tiles):
                    if t >= 2:
                        sp.wait_ge(turned, 2 * (t - 1))
                    sp.dma_start(xt[0:m, t % 2, :], rows_of(t)).then_inc(x_in[t % 2], 16)

            @block.scalar
            def _(act):
                for t, (r0, m) in enumerate(tiles):
                    act.wait_ge(x_in[t % 2], 16 * (t // 2 + 1))
                    if t >= 1:
                        act.wait_ge(squared, t)
                    if t >= 2:
                        act.wait_ge(scaled, 2 * (t - 1))
                    act.activation(junk[0:m, :], xt[0:m, t % 2, :], ACT.Square,
                                   accum_out=ss[0:m, 0, t % 2:t % 2 + 1]).then_inc(squared, 1)
                    act.wait_ge(meaned, t + 1)
                    act.activation(ss[0:m, 2, t % 2:t % 2 + 1], ss[0:m, 1, t % 2:t % 2 + 1],
                                   ACT.Sqrt).then_inc(rooted, 1)

            @block.vector
            def _(dve):
                dve.wait_ge(gain_turned, 1)
                dve.tensor_copy(gcol[:, :], ps[3][:, 0, 0:DK]).then_inc(gain_ready, 1)
                dve.wait_ge(gain_ready, 1)

                def copy_out(t):
                    r0, m = tiles[t]
                    for j in range(2):
                        dve.wait_ge(turned, 2 * t + j + 1)
                        dve.tensor_tensor(out_T[:, 4 * j:4 * j + 4, r0:r0 + m], ps[(2 * t + j) % 4][:, :, 0:m],
                                          wide(gcol[:, 4 * j:4 * j + 4], m), ALU.mult).then_inc(copied, 1)

                for t, (r0, m) in enumerate(tiles):
                    s = t % 2
                    dve.wait_ge(squared, t + 1)
                    dve.tensor_scalar(ss[0:m, 1, s:s + 1], ss[0:m, 0, s:s + 1], 1.0 / D, EPS,
                                      ALU.mult, ALU.add).then_inc(meaned, 1)
                    if t >= 1:
                        copy_out(t - 1)
                    dve.wait_ge(rooted, t + 1)
                    dve.reciprocal(ss[0:m, 3, s:s + 1], ss[0:m, 2, s:s + 1]).then_inc(scaled, 1)
                    dve.wait_ge(scaled, 2 * t + 1)
                    dve.tensor_scalar(xt[0:m, s, :], xt[0:m, s, :], ss[0:m, 3, s:s + 1], None,
                                      ALU.mult).then_inc(scaled, 1)
                copy_out(n - 1)

            @block.tensor
            def _(pe):
                pe.wait_ge(gain_in, 16)
                pe.transpose(ps[3][:, 0, 0:DK], grow[:, :], ident[0:DK, 0:DK]).then_inc(gain_turned, 1)
                pe.wait_ge(gain_ready, 1)
                for t, (r0, m) in enumerate(tiles):
                    pe.wait_ge(scaled, 2 * t + 2)
                    for j in range(2):
                        u = 2 * t + j
                        if u >= 4:
                            pe.wait_ge(copied, u - 3)
                        for k in range(4):
                            mm = pe.transpose(ps[u % 4][:, k, 0:m], xt[0:m, t % 2, (4 * j + k) * P:(4 * j + k + 1) * P],
                                              ident[0:m, 0:m])
                        mm.then_inc(turned, 1)


def project_in(nc, u_T, w_in, proj):
    chunk = 408
    chunks = C_MG // chunk
    assert chunk * chunks == C_MG and chunks % 2 == 0
    nt = len(TILES)
    ring = 6
    with Stage(nc, "pin") as st:
        w = st.sb("w", [P, 2, DK, chunk])
        ob = st.sb("ob", [P, ring, chunk])
        ps = [st.ps(f"ps{i}", [P, 512]) for i in range(ring)]
        w_in_sem = [st.sem("w0_in"), st.sem("w1_in")]
        product = st.sem("product")
        by_act, by_dve = st.sem("copied_act"), st.sem("copied_dve")
        stored = [st.sem(f"stored{i}") for i in range(ring)]
        w_k = w_in.rearrange("(k p) n -> p k n", p=P)
        per = 2 * nt
        half = per // 2

        with nc.Block() as block:
            @block.tensor
            def _(pe):
                with pe.Fori(0, chunks // 2) as it:
                    for s in range(2):
                        pe.wait_ge(w_in_sem[s], it * 16 + 16)
                        for t, (r0, m) in enumerate(TILES):
                            u = s * nt + t
                            pe.wait_ge(by_dve if u % 2 else by_act, it * half + (u // 2 + 1))
                            for k in range(DK):
                                mm = pe.matmul(ps[u % ring][0:m, 0:chunk], u_T[:, k, r0:r0 + m], w[:, s, k, :],
                                               start=(k == 0), stop=(k == DK - 1))
                            mm.then_inc(product, 1)

            def copy_out(eng, it, u, copied):
                m = TILES[u % nt][1]
                eng.wait_ge(product, it * per + (u + 1))
                eng.wait_ge(stored[u % ring], it * (16 * per // ring) + 16 * (u // ring + 1))
                if eng is nc.scalar:
                    eng.copy(ob[0:m, u % ring, :], ps[u % ring][0:m, 0:chunk]).then_inc(copied, 1)
                else:
                    eng.tensor_copy(ob[0:m, u % ring, :], ps[u % ring][0:m, 0:chunk]).then_inc(copied, 1)

            @block.scalar
            def _(act):
                act.sem_inc(by_act, ring // 2)
                with act.Fori(0, chunks // 2) as it:
                    for u in range(0, per, 2):
                        copy_out(act, it, u, by_act)

            @block.vector
            def _(dve):
                dve.sem_inc(by_dve, ring // 2)
                with dve.Fori(0, chunks // 2) as it:
                    for u in range(1, per, 2):
                        copy_out(dve, it, u, by_dve)

            @block.sync
            def _(sp):
                for s in range(ring):
                    sp.sem_inc(stored[s], 16)
                for s in range(2):
                    sp.dma_start(w[:, s], w_k[:, :, s * chunk:(s + 1) * chunk]).then_inc(w_in_sem[s], 16)

                def store_chunk(it, s):
                    for t, (r0, m) in enumerate(TILES):
                        u = s * nt + t
                        sp.wait_ge(by_dve if u % 2 else by_act, it * half + (u // 2 + 1 + ring // 2))
                        cols = bass.ds((it * 2 + s) * chunk, chunk)
                        sp.dma_start(proj[r0:r0 + m, cols], ob[0:m, u % ring, :]).then_inc(stored[u % ring], 16)

                last = chunks // 2 - 1
                with sp.Fori(0, last) as it:
                    for s in range(2):
                        store_chunk(it, s)
                        sp.dma_start(w[:, s], w_k[:, :, bass.ds((it * 2 + 2 + s) * chunk, chunk)]).then_inc(w_in_sem[s], 16)
                for s in range(2):
                    store_chunk(last, s)
                for s in range(ring):
                    sp.wait_ge(stored[s], 16 * (1 + per * (chunks // 2) // ring))


def cache_moves(ins, proj, outs):
    moves = []
    kv = slice(C_KV, C_KV + 4 * KVH * DH)
    win = slice(C_KV + 4 * KVH * DH, C_KV + 6 * KVH * DH)

    def flat(ap):
        return ap.rearrange("l b r s h d -> (l b) r (s h d)")

    moves.append((outs["nsa_kv_prompt"].rearrange("l b r s h d -> (l b r) (s h d)"), proj[0:SEQ, kv]))
    moves.append((outs["nsa_kv_sample"].rearrange("l b r s h d -> (l b r) (s h d)"), proj[SEQ:TOK, kv]))
    moves.append((flat(outs["nsa_win_prompt"])[0], proj[SEQ - WIN:SEQ, win]))
    o = flat(outs["nsa_win_sample"])
    for b in range(DB):
        moves.append((o[b, WIN - DT:WIN, :], proj[SEQ + b * DT:SEQ + (b + 1) * DT, win]))
    xbc = slice(C_XBC, C_XBC + SCD)
    moves.append((outs["ssd_conv_prompt"][0, 0], proj[SEQ - SCONV + 1:SEQ, xbc]))
    xs = proj[SEQ:TOK, xbc].rearrange("(b t) c -> b t c", t=DT)
    moves.append((outs["ssd_conv_sample"][0], xs[:, DT - SCONV + 1:DT, :]))
    for g, (w, d) in enumerate(DIL):
        r = min(w, PAST)
        o = outs[f"dil{w}_prompt"][0, 0].rearrange("r s h d -> r s (h d)")
        for s in range(2):
            c = C_DIL + (1 + s) * DILH * DH + g * DG * DH
            rows = min(r, SEQ)
            moves.append((o[r - rows:r, s, :], proj[SEQ - rows:SEQ, c:c + DG * DH]))
            for b in range(DB):
                moves.append((outs[f"dil{w}_sample"][0, b, r - DT:r, s].rearrange("r h d -> r (h d)"),
                              proj[SEQ + b * DT:SEQ + (b + 1) * DT, c:c + DG * DH]))
    moves.append((outs["dil2048_prompt"][0, 0, 0:PAST - SEQ].rearrange("(p a) s h d -> p (a s h d)", p=P), ins["k_pad"]))
    for name, w in (("nsa_win", WIN),) + tuple((f"dil{w}", w) for w, _ in DIL):
        src = ins["cache_nsa_win" if name == "nsa_win" else f"cache_dil_w{w}"]
        s = src.rearrange("l b r s h d -> (l b) (r s h d)")
        o = outs[f"{name}_sample"].rearrange("l b r s h d -> (l b) (r s h d)")
        row = s.shape[1] // w
        for b in range(DB):
            moves.append((o[b, 0:(w - DT) * row].rearrange("(a c) -> a c", a=w - DT),
                          s[b, DT * row:w * row].rearrange("(a c) -> a c", a=w - DT)))
    return moves


def attention(nc, st, iters, preps, tasks, heads, scale_tables, ident, inputs_in, programs, stored_per_iter):
    nt, nh = len(tasks), heads
    per_head = nt // nh
    assert per_head * nh == nt and nt % 2 == 0 and nh % 2 == 0
    group_of, n_groups = [], len(preps)
    for task in tasks:
        tiles = len(task["v"])
        group_of.append([(n_groups + i, 4 * i, min(tiles, 4 * i + 4)) for i in range(-(-tiles // 4))])
        n_groups += len(group_of[-1])
    assert n_groups % 2 == 0
    nk_max = max(task["k"].shape[1] for task in tasks)
    banks = -(-nk_max // 512)

    probs = st.sb("probs", [P, 2, nk_max])
    probs_T = st.sb("probs_T", [P, 2, max(len(task["v"]) for task in tasks) * P])
    row_max = st.sb("row_max", [P, nt])
    neg_all = st.sb("neg_max", [P, nt])
    sum_all = st.sb("row_sum", [P, nt])
    inverse = st.sb("inverse", [P, nt])
    S = [st.ps(f"S{i}", [P, 512 * banks]) for i in range(2)]
    T = [st.ps(f"T{i}", [P, 4, P]) for i in range(2)]
    O = [st.ps(f"O{i}", [P, 512]) for i in range(2)]
    scores, biased, shifted = st.sem("scores"), st.sem("biased"), st.sem("shifted")
    exped, turned, pv = st.sem("exped"), st.sem("turned"), st.sem("pv")
    copied = [st.sem("copied_act"), st.sem("copied_dve")]
    inverted, normalised = st.sem("inverted"), st.sem("normalised")
    tables, stored, aside = st.sem("tables"), st.sem("stored"), st.sem("aside")
    credit = 2 * per_head
    sems = dict(turned=turned, pv=pv, normalised=normalised, stored=stored, inverted=inverted)
    info = dict(nt=nt, n_groups=n_groups, preps=len(preps))

    def neg_max(n):
        return tasks[n]["stats"][0] if "stats" in tasks[n] else neg_all[:, n:n + 1]

    def row_sum(n):
        return tasks[n]["stats"][1] if "stats" in tasks[n] else sum_all[:, n:n + 1]

    def turn(pe, it, g, parts):
        pe.wait_ge(copied[g % 2], it * (n_groups // 2) + (g // 2 + 1))
        if parts[0][0].shape[1] < P:
            stand(pe, aside)
        for i, (src, m) in enumerate(parts):
            mm = pe.transpose(T[g % 2][0:src.shape[-1] if len(src.shape) == 2 else P, i, 0:m], src, ident[0:m, 0:m])
        mm.then_inc(turned, 1)

    def copy_group(eng, it, g, out, src):
        eng.wait_ge(turned, it * n_groups + (g + 1))
        if g % 2 == 0:
            eng.copy(out, src).then_inc(copied[0], 1)
        else:
            eng.tensor_copy(out, src).then_inc(copied[1], 1)

    def copy_preps(eng, it, side):
        for g, (parts, target, m) in enumerate(preps):
            if g % 2 == side:
                copy_group(eng, it, g, target, T[g % 2][:, 0:len(parts), 0:m])

    def copy_probs(eng, it, n, side):
        for g, a, b in group_of[n]:
            if g % 2 == side:
                eng.wait_ge(pv, it * nt + (n + 1))
                keys = max(v.shape[0] for v in tasks[n]["v"][a:b])
                copy_group(eng, it, g, probs_T[0:keys, n % 2, a * P:b * P].rearrange("k (t q) -> k t q", q=P),
                           T[g % 2][0:keys, 0:b - a, :])

    with nc.Block() as block:
        @block.tensor
        def _(pe):
            def score(it, n):
                task = tasks[n]
                pe.wait_ge(biased, it * nt + (n + credit - 1))
                nk = task["k"].shape[1]
                for c in range(0, nk, 512):
                    e = min(nk, c + 512)
                    mm = pe.matmul(S[n % 2][:, c:e], task["q"], task["k"][:, c:e], start=True, stop=True)
                mm.then_inc(scores, 1)

            with pe.Fori(0, iters) as it:
                inputs_in(pe, it)
                for g, (parts, target, m) in enumerate(preps):
                    turn(pe, it, g, [(s, m) for s in parts])
                for side in range(2):
                    pe.wait_ge(copied[side], it * (n_groups // 2) + ((len(preps) + 1 - side) // 2 + 1))
                score(it, 0)
                for n, task in enumerate(tasks):
                    if n + 1 < nt:
                        score(it, n + 1)
                    pe.wait_ge(exped, it * nt + (n + 1))
                    col = 0
                    for g, a, b in group_of[n]:
                        parts = []
                        for v in task["v"][a:b]:
                            parts.append((probs[:, n % 2, col:col + v.shape[0]], P))
                            col += v.shape[0]
                        turn(pe, it, g, parts)
                    for side in range(2):
                        own = [g for g, _, _ in group_of[n] if g % 2 == side]
                        if own:
                            pe.wait_ge(copied[side], it * (n_groups // 2) + (own[-1] // 2 + 2))
                    pe.wait_ge(normalised, it * nt + (n + 1))
                    for i, v in enumerate(task["v"]):
                        mm = pe.matmul(O[n % 2][:, 0:DH], probs_T[0:v.shape[0], n % 2, i * P:(i + 1) * P], v,
                                       start=(i == 0), stop=(i == len(task["v"]) - 1))
                    mm.then_inc(pv, 1)

        @block.scalar
        def _(act):
            act.sem_inc(copied[0], 1)
            with act.Fori(0, iters) as it:
                copy_preps(act, it, 0)
                for n, task in enumerate(tasks):
                    nk = task["k"].shape[1]
                    act.wait_ge(shifted, it * nt + (n + 1))
                    act.activation(probs[:, n % 2, 0:nk], probs[:, n % 2, 0:nk], ACT.Exp, scale=DH ** -0.5,
                                   bias=neg_max(n), accum_out=row_sum(n)).then_inc(exped, 1)
                    copy_probs(act, it, n, 0)

        @block.vector
        def _(dve):
            dve.sem_inc(copied[1], 1)
            dve.sem_inc(biased, credit)
            dve.sem_inc(pv, 2)
            dve.sem_inc(normalised, 2)

            def bias(it, n):
                task = tasks[n]
                nk = task["k"].shape[1]
                dve.wait_ge(scores, it * nt + (n + 1))
                dve.wait_ge(pv, it * nt + (n + 1))
                stand(dve, aside)
                dve.tensor_tensor_reduce(probs[:, n % 2, 0:nk], S[n % 2][:, 0:nk], task["table"](task["head"] % 2),
                                         1.0, -3.0e38, ALU.add, ALU.max, row_max[:, n:n + 1]).then_inc(biased, 1)
                dve.wait_ge(biased, it * nt + (n + credit + 1))
                dve.tensor_scalar(neg_max(n), row_max[:, n:n + 1], -1.0e20, -(DH ** -0.5),
                                  ALU.max, ALU.mult).then_inc(shifted, 1)

            with dve.Fori(0, iters) as it:
                copy_preps(dve, it, 1)
                dve.wait_ge(stored, it * (16 * stored_per_iter) + 16 * stored_per_iter)
                for n, task in enumerate(tasks):
                    if n % per_head == 0:
                        dve.wait_ge(tables, it * nh + (task["head"] + 1))
                    if n == 0:
                        bias(it, 0)
                    if n + 1 < nt:
                        if (n + 1) % per_head == 0:
                            dve.wait_ge(tables, it * nh + (tasks[n + 1]["head"] + 1))
                        bias(it, n + 1)
                    copy_probs(dve, it, n, 1)
                    dve.wait_ge(exped, it * nt + (n + 1))
                    dve.tensor_scalar(inverse[:, n:n + 1], row_sum(n), 1.0e-30, None, ALU.max).then_inc(inverted, 1)
                    dve.wait_ge(inverted, it * (2 * nt) + (2 * n + 1))
                    dve.reciprocal(inverse[:, n:n + 1], inverse[:, n:n + 1]).then_inc(inverted, 1)
                    dve.wait_ge(inverted, it * (2 * nt) + (2 * n + 2))
                    dve.wait_ge(pv, it * nt + (n + 3))
                    dve.tensor_scalar(task["out"], O[n % 2][:, 0:DH], inverse[:, n:n + 1], None,
                                      ALU.mult).then_inc(normalised, 1)

        @block.gpsimd
        def _(pool):
            with pool.Fori(0, iters) as it:
                inputs_in(pool, it)
                for j in range(nh):
                    pool.wait_ge(biased, it * nt + per_head * (j + 1))
                    stand(pool, aside)
                    scale_tables(pool, j, j % 2).then_inc(tables, 1)

        @block.sync
        def _(sp):
            sp.sem_inc(stored, 16 * stored_per_iter)
            programs(sp, sems, info)


def nsa_prompt(nc, ins, proj, kc_T, vc, o_cmp, o_sel, o_win, ident, moves, moved):
    assert SEQ // SEL_L <= SEL_N
    with Stage(nc, "nsap") as st:
        q_raw = st.sb("q_raw", [P, 2, PT, P])
        k_raw = st.sb("k_raw", [P, 2, PT, 2 * DH])
        q_T = st.sb("q_T", [P, 2, SEQ])
        k_T = st.sb("k_T", [P, 2, SEQ])
        kc = st.sb("kc", [P, NCMP_P])
        v = st.sb("v", [P, 2, PT, DH])
        vcs = st.sb("vcs", [NCMP_P, DH])
        out = st.sb("out", [P, 2, 3, PT, P])
        wc, ww, wx = SEQ, WIN + P, PT * NCMP_P
        tab = st.sb("tab", [P, wc + ww + wx])
        slopes = st.sb("slopes", [P, NSA_R])
        scaled = st.sb("scaled", [P, 2, wc + ww + wx])
        raw_in, kv_in, tab_in = st.sem("raw_in"), st.sem("kv_in"), st.sem("tab_in")

        preps = []
        for b in range(2):
            for a in range(0, PT, 4):
                preps.append(([k_raw[:, b, t, :] for t in range(a, a + 4)],
                              k_T[:, b, a * P:(a + 4) * P].rearrange("d (t k) -> d t k", k=P), P))
        for pair in range(2):
            for a in range(0, PT, 4):
                preps.append(([q_raw[:, pair, t, :] for t in range(a, a + 4)],
                              q_T[:, pair, a * P:(a + 4) * P].rearrange("d (t k) -> d t k", k=P), P))

        tasks = []
        for pair in range(2):
            for hh in range(2):
                r = slice(hh * DH, (hh + 1) * DH)
                for i in range(PT):
                    q = q_T[r, pair, i * P:(i + 1) * P]

                    def add(br, k, c0, vs):
                        nk = k.shape[1]
                        tasks.append(dict(q=q, k=k, head=2 * pair + hh, v=vs,
                                          table=lambda s, c0=c0, nk=nk: scaled[:, s, c0:c0 + nk],
                                          out=out[:, pair, br, i, hh * DH:(hh + 1) * DH]))
                    add(1, k_T[r, 0, 0:(i + 1) * P], (PT - 1 - i) * P, [v[:, 0, t, :] for t in range(i + 1)])
                    t0 = max(0, i - WIN // P)
                    add(2, k_T[r, 1, t0 * P:(i + 1) * P], wc + (WIN // P - (i - t0)) * P,
                        [v[:, 1, t, :] for t in range(t0, i + 1)])
                    add(0, kc[r, :], wc + ww + i * NCMP_P, [vcs[:, :]])

        def inputs_in(eng, it):
            eng.wait_ge(kv_in, it * (16 * 7) + 16 * 7)
            if eng is nc.gpsimd:
                eng.wait_ge(tab_in, 16)
            else:
                eng.wait_ge(raw_in, it * (16 * 6) + 16 * 6)

        def scale_tables(pool, j, slot):
            return pool.tensor_scalar(scaled[:, slot, :], tab[:, :], slopes[:, j:j + 1], None, ALU.mult)

        def tok(c0, n):
            return proj[0:SEQ, c0:c0 + n].rearrange("(t p) c -> p t c", p=P)

        def programs(sp, sems, info):
            kcol = C_KV + np.array([2, 4]) * KVH * DH
            sp.dma_start(tab[:, :], ins["k_nsa_tab"]).then_inc(tab_in, 16)

            def load_raw(g):
                for b in range(2):
                    for dup in range(2):
                        sp.dma_start(k_raw[:, b, :, dup * DH:(dup + 1) * DH], tok(int(kcol[b]) + g * DH, DH)).then_inc(raw_in, 16)
                for pair in range(2):
                    sp.dma_start(q_raw[:, pair], tok(C_Q + (2 * g + pair) * P, P)).then_inc(raw_in, 16)

            def load_kv(g):
                for b in range(2):
                    sp.dma_start(v[:, b], tok(int(kcol[b]) + KVH * DH + g * DH, DH)).then_inc(kv_in, 16)
                for dup in range(2):
                    sp.dma_start(kc[dup * DH:(dup + 1) * DH, :], kc_T[DB, g * DH:(g + 1) * DH, 0:NCMP_P]).then_inc(kv_in, 16)
                sp.dma_start(vcs[:, :], vc[DB, 0:NCMP_P, g * DH:(g + 1) * DH]).then_inc(kv_in, 16)
                for h in range(2):
                    sp.dma_start(slopes[:, 2 * h:2 * h + 2], ins["k_nsa_slopes"][:, g * NSA_R + 2 * h:g * NSA_R + 2 * h + 2]).then_inc(kv_in, 16)

            def store(g, pair):
                sp.wait_ge(sems["normalised"], 2 + info["nt"] * g + info["nt"] // 2 * (pair + 1))
                for br, o in enumerate((o_cmp, o_sel, o_win)):
                    c = (2 * g + pair) * P
                    sp.dma_start(o[0:SEQ, c:c + P].rearrange("(t p) c -> p t c", p=P), out[:, pair, br]).then_inc(sems["stored"], 16)

            load_raw(0)
            load_kv(0)
            sp.wait_ge(sems["turned"], info["preps"])
            load_raw(1)
            for target, source in moves:
                sp.dma_start(target, source).then_inc(moved, 16)
            store(0, 0)
            store(0, 1)
            sp.wait_ge(sems["pv"], 2 + info["nt"])
            load_kv(1)
            store(1, 0)
            store(1, 1)
            sp.wait_ge(sems["stored"], 16 * 6 * 3)

        attention(nc, st, KVH, preps, tasks, NSA_R, scale_tables, ident, inputs_in, programs, 6)


def dil_prompt(nc, ins, proj, o_dil, ident):
    with Stage(nc, "dilp") as st:
        rounds = DILH // 2
        q_raw = st.sb("q_raw", [P, PT, P])
        k_raw = st.sb("k_raw", [P, PT, P])
        q_T = st.sb("q_T", [P, SEQ])
        k_T = st.sb("k_T", [P, P + SEQ])
        out = st.sb("out", [P, PT, DCOL])
        tab = st.sb("tab", [P, 3, 2 * P])
        slopes = st.sb("slopes", [P, 2])
        scaled = st.sb("scaled", [P, 2, 3, 2 * P])
        raw_in, kv_in, cleared = st.sem("raw_in"), st.sem("kv_in"), st.sem("cleared")
        v = st.sb("v", [P, PT + 1, P])

        preps = []
        for src, dst, c0 in ((k_raw, k_T, P), (q_raw, q_T, 0)):
            for a in range(0, PT, 4):
                preps.append(([src[:, t, :] for t in range(a, a + 4)],
                              dst[:, c0 + a * P:c0 + (a + 4) * P].rearrange("d (t k) -> d t k", k=P), P))
        tasks = []
        for hh in range(2):
            r = slice(hh * DH, (hh + 1) * DH)
            for t in range(PT):
                kind = 0 if t == 0 else 2 - t % 2
                tasks.append(dict(q=q_T[r, t * P:(t + 1) * P], k=k_T[r, t * P:(t + 2) * P], head=hh,
                                  table=lambda s, kind=kind: scaled[:, s, kind, :],
                                  v=[v[:, t + e, hh * DH:(hh + 1) * DH] for e in range(2)],
                                  out=out[:, t, hh * DH:(hh + 1) * DH],
                                  stats=(out[:, t, P + hh:P + hh + 1], out[:, t, P + 2 + hh:P + 3 + hh])))

        def inputs_in(eng, it):
            eng.wait_ge(cleared, 2)
            eng.wait_ge(kv_in, it * 48 + 48)
            if eng is nc.tensor:
                eng.wait_ge(raw_in, it * 32 + 32)

        def scale_tables(pool, j, slot):
            return pool.tensor_scalar(scaled[:, slot], tab[:, :, :], slopes[:, j:j + 1], None, ALU.mult)

        def folded(ap, d):
            if d == 1:
                return [(slice(0, P), slice(0, PT), ap.rearrange("(t p) c -> p t c", p=P))]
            per = SEQ // d
            if per >= P:
                k = per // P
                x = ap.rearrange("(k p r) c -> r k p c", p=P, r=d)
                return [(slice(0, P), slice(r * k, (r + 1) * k), x[r].rearrange("k p c -> p k c")) for r in range(d)]
            k = P // per
            x = ap.rearrange("(i r) c -> r i c", r=d)
            return [(slice((r % k) * per, (r % k + 1) * per), r // k, x[r]) for r in range(d)]

        def programs(sp, sems, info):
            landed = st.sem("landed")
            count = 0

            def move(tile, ap, d, load):
                n = 0
                for ps, ts, rows in folded(ap, d):
                    dst = tile[ps, ts, :]
                    if load:
                        sp.dma_start(dst, rows).then_inc(landed, 16)
                    else:
                        sp.dma_start(rows, dst).then_inc(landed, 16)
                    n += 16
                return n

            for n in range(rounds):
                g, pair = n // 2, n % 2
                d = DIL[g][1]
                h0 = 2 * n
                if n >= 1:
                    sp.wait_ge(sems["turned"], (n - 1) * info["n_groups"] + info["preps"])
                for raw, which in ((k_raw, 1), (q_raw, 0)):
                    c = C_DIL + which * DILH * DH + h0 * DH
                    count += move(raw, proj[0:SEQ, c:c + P], d, True)
                sp.wait_ge(landed, count)
                sp.sem_inc(raw_in, 32)
                if n >= 1:
                    sp.wait_ge(sems["pv"], 2 + n * info["nt"])
                    sp.wait_ge(sems["normalised"], 2 + n * info["nt"])
                    gp, pp = (n - 1) // 2, (n - 1) % 2
                    count += store(move, gp, pp)
                c = C_DIL + 2 * DILH * DH + h0 * DH
                count += move(v[:, 1:PT + 1, :], proj[0:SEQ, c:c + P], d, True)
                sp.dma_start(tab[:, :, :], ins["k_dil_tab"][g]).then_inc(landed, 16)
                sp.dma_start(slopes[:, :], ins["k_dil_slopes"][:, h0:h0 + 2], ).then_inc(landed, 16)
                count += 32
                sp.wait_ge(landed, count)
                sp.sem_inc(kv_in, 48)
                if n >= 1:
                    sp.sem_inc(sems["stored"], 16)
            sp.wait_ge(sems["normalised"], 2 + rounds * info["nt"])
            count += store(move, (rounds - 1) // 2, (rounds - 1) % 2)
            sp.wait_ge(landed, count)

        def store(move, g, pair):
            return move(out, o_dil[g, 0:SEQ, pair], DIL[g][1], False)

        with nc.Block() as block:
            @block.gpsimd
            def _(pool):
                pool.memset(k_T[:, 0:P], 0.0).then_inc(cleared, 1)
                pool.memset(v[:, 0, :], 0.0).then_inc(cleared, 1)

        attention(nc, st, rounds, preps, tasks, 2, scale_tables, ident, inputs_in, programs, 1)


def nsa_compress(nc, ins, proj, kc_T, vc, ident):
    assert (NCMP + 1) * CMP_S <= PAST and CMP_L == 2 * CMP_S
    seqs = DB + 1
    LP = CMP_S // 2
    cols = 2 * KVH * DH
    per_page = PAGE // CMP_S
    with Stage(nc, "cmp") as st:
        rows = st.sb("rows", [P, 2, CMP_S, cols])
        packed = st.sb("packed", [P, 2, 2 * KVH, CMP_S * DH])
        rows_T = st.sb("rows_T", [P, 2 * KVH * LP, P])
        w1 = st.sb("w1", [P, 2, 2 * LP, HID])
        w2 = st.sb("w2", [P, 2, DH])
        pe_raw = st.sb("pe_raw", [2 * 2 * LP, P])
        pe_T = st.sb("pe_T", [P, 2 * 2 * LP])
        bias = st.sb("bias", [P, 2])
        gate = st.sb("gate", [P, 2, KVH, P])
        hid = st.sb("hid", [P, 2, KVH, P])
        out = st.sb("out", [P, 2, P])
        pages = st.sb("pages", [1, DB * NPAGES], I32)
        T = [st.ps(f"T{i}", [P, 4, P]) for i in range(4)]
        H = [st.ps(f"H{i}", [P, KVH, P]) for i in range(2)]
        O = [st.ps(f"O{i}", [P, P]) for i in range(2)]
        const_in, rows_in = st.sem("const_in"), [st.sem("rows_in0"), st.sem("rows_in1")]
        turned, packs = st.sem("turned"), st.sem("packs")
        copied = [st.sem("copied_act"), st.sem("copied_dve")]
        hidden, gated, acted = st.sem("hidden"), st.sem("gated"), st.sem("acted")
        outs_made, outs_copied = st.sem("outs_made"), st.sem("outs_copied")
        stored = [st.sem("stored_k"), st.sem("stored_v")]
        setup, aside = st.sem("setup"), st.sem("aside")

        with nc.Block() as block:
            @block.sync
            def _(sp):
                sp.dma_start(w1[:, :, :, :], ins["nsa_cmp_w1"][0].rearrange("s (l p) h -> p s l h", p=P)).then_inc(const_in, 16)
                sp.dma_start(w2[:, :, :], ins["nsa_cmp_w2"][0].rearrange("s h d -> h s d")).then_inc(const_in, 16)
                sp.dma_start(pe_raw[:, :], ins["nsa_pe"][0].rearrange("s (l r) d -> (s l) (r d)", r=2)).then_inc(const_in, 16)
                sp.dma_start(pages[:, :], ins["page_table"].rearrange("(o b) n -> o (b n)", o=1)).then_inc(const_in, 16)

            @block.tensor
            def _(pe):
                pe.wait_ge(const_in, 64)
                pe.transpose(T[0][:, 0, 0:4 * LP], pe_raw[:, :], ident[0:4 * LP, 0:4 * LP]).then_inc(setup, 1)
                pe.wait_ge(setup, 2)
                for s in range(2):
                    for l in range(2 * LP):
                        mm = pe.matmul(H[s][:, 0, 0:1], w1[:, s, l, :], pe_T[:, s * 2 * LP + l:s * 2 * LP + l + 1],
                                       start=(l == 0), stop=(l == 2 * LP - 1))
                mm.then_inc(setup, 1)

            @block.vector
            def _(dve):
                dve.wait_ge(setup, 1)
                dve.tensor_copy(pe_T[:, :], T[0][:, 0, 0:4 * LP]).then_inc(setup, 1)
                dve.wait_ge(setup, 3)
                for s in range(2):
                    dve.tensor_copy(bias[:, s:s + 1], H[s][:, 0, 0:1]).then_inc(setup, 1)

        def groups(g):
            s, h = divmod(g // 2, KVH)
            return s, h, 4 * (g % 2)

        def copy_group(eng, n, g, m):
            s, h, l0 = groups(g)
            eng.wait_ge(turned, n * 8 + (16 + g + 1))
            eng.wait_ge(hidden, n * 2 + 2)
            dst = rows_T[:, (s * KVH + h) * LP + l0:(s * KVH + h) * LP + l0 + 4, 0:m]
            if g % 2 == 0:
                eng.copy(dst, T[g % 4][:, :, 0:m]).then_inc(copied[0], 1)
            else:
                eng.tensor_copy(dst, T[g % 4][:, :, 0:m]).then_inc(copied[1], 1)

        def pe_seq(pe, n, slot, m, blocks):
            for g in range(8):
                s, h, l0 = groups(g)
                pe.wait_ge(copied[g % 2], n * 4 + (g // 2 + 1))
                for i in range(4):
                    l = 2 * (l0 + i)
                    mm = pe.transpose(T[g % 4][:, i, 0:m], packed[0:m, slot, s * KVH + h, l * DH:(l + 2) * DH],
                                      ident[0:m, 0:m])
                mm.then_inc(turned, 1)
            for s in range(2):
                for side in range(2):
                    pe.wait_ge(copied[side], n * 4 + (2 + 2 * (s + 1)))
                pe.wait_ge(acted, n * 2 + (s + 1))
                for l in range(2 * LP):
                    j, lp = divmod(l, LP)
                    r0 = s * KVH * LP + lp
                    mm = pe.matmul(H[s][:, :, 0:blocks], w1[:, s, l, :], rows_T[:, r0:r0 + (KVH - 1) * LP + 1:LP, j:j + blocks],
                                   start=(l == 0), stop=(l == 2 * LP - 1))
                mm.then_inc(hidden, 1)
            for s in range(2):
                pe.wait_ge(acted, n * 2 + (2 + s + 1))
                pe.wait_ge(outs_copied, n * 2 + (s + 1))
                for h in range(KVH):
                    if s == 0:
                        mm = pe.matmul(O[s][h * DH:(h + 1) * DH, 0:blocks], w2[:, s, :], hid[:, s, h, 0:blocks],
                                       start=True, stop=True)
                    else:
                        mm = pe.matmul(O[s][0:blocks, h * DH:(h + 1) * DH], hid[:, s, h, 0:blocks], w2[:, s, :],
                                       start=True, stop=True)
                mm.then_inc(outs_made, 1)

        def act_seq(act, n, m, blocks):
            for g in range(0, 8, 2):
                copy_group(act, n, g, m)
            for s in range(2):
                act.wait_ge(hidden, n * 2 + (2 + s + 1))
                act.wait_ge(acted, n * 2 + (s + 1))
                act.activation(gate[:, s, :, 0:blocks], H[s][:, :, 0:blocks], ACT.Sigmoid,
                               bias=bias[:, s:s + 1]).then_inc(gated, 1)
            for s in range(2):
                act.wait_ge(outs_copied, n * 2 + (2 + s + 1))
                dst = kc_T if s == 0 else vc
                src = out[:, 0, 0:blocks] if s == 0 else out[0:blocks, 1, :]
                d = dst[bass.ds(n, 1)] if not isinstance(n, int) else dst[n:n + 1]
                d = d[:, :, 0:blocks] if s == 0 else d[:, 0:blocks, :]
                act.dma_start(d.rearrange("o p c -> (o p) c"), src).then_inc(stored[s], 16)

        def dve_seq(dve, n, m, blocks):
            for g in range(1, 8, 2):
                copy_group(dve, n, g, m)
            for s in range(2):
                dve.wait_ge(gated, n * 2 + (s + 1))
                dve.wait_ge(outs_made, n * 2 + (s + 1))
                dve.scalar_tensor_tensor(hid[:, s, :, 0:blocks], H[s][:, :, 0:blocks], bias[:, s:s + 1],
                                         gate[:, s, :, 0:blocks], ALU.add, ALU.mult).then_inc(acted, 1)
            for s in range(2):
                dve.wait_ge(outs_made, n * 2 + (2 + s + 1))
                dve.wait_ge(stored[s], n * 16 + 16)
                a = (slice(0, P), slice(0, blocks)) if s == 0 else (slice(0, blocks), slice(0, P))
                dve.tensor_copy(out[a[0], s, a[1]], O[s][a[0], a[1]]).then_inc(outs_copied, 1)

        def pack(pool, n, slot, m):
            pool.wait_ge(turned, n * 8 + 8)
            stand(pool, aside)
            pool.tensor_copy(packed[0:m, slot].rearrange("p h (l d) -> p l h d", d=DH),
                             rows[0:m, slot].rearrange("p l (h d) -> p l h d", d=DH)).then_inc(packs, 1)

        with nc.Block() as block:
            @block.gpsimd
            def _(pool):
                pool.sem_inc(packs, 2)
                with pool.Fori(0, DB // 2) as it:
                    for slot in range(2):
                        pool.wait_ge(rows_in[slot], it * (16 * NPAGES) + 16 * NPAGES)
                        pack(pool, it * 2 + slot, slot, P)
                pool.wait_ge(rows_in[0], 16 * NPAGES * DB // 2 + 16)
                pack(pool, DB, 0, SEQ // CMP_S)

            @block.sync
            def _(sp):
                sp.sem_inc(turned, 16)
                with sp.Fori(0, DB // 2) as it:
                    for slot in range(2):
                        sp.wait_ge(packs, it * 2 + (slot + 1))
                        for j in range(NPAGES):
                            page = sp.value_load(pages[0:1, bass.ds((it * 2 + slot) * NPAGES + j, 1)],
                                                 min_val=0, max_val=ins["cache_nsa_kv"].shape[1] - 1)
                            src = ins["cache_nsa_kv"][0, bass.ds(page, 1)].rearrange("o (c l) s h d -> (o c) l (s h d)", l=CMP_S)
                            sp.dma_start(rows[j * per_page:(j + 1) * per_page, slot], src[:, :, 0:cols]).then_inc(rows_in[slot], 16)
                sp.wait_ge(packs, DB + 1)
                sp.dma_start(rows[0:SEQ // CMP_S, 0], proj[0:SEQ, C_KV:C_KV + cols].rearrange("(c l) k -> c l k", l=CMP_S)).then_inc(rows_in[0], 16)

            @block.tensor
            def _(pe):
                pe.sem_inc(hidden, 2)
                pe.sem_inc(outs_made, 2)
                with pe.Fori(0, DB // 2) as it:
                    for slot in range(2):
                        pe.wait_ge(packs, it * 2 + (slot + 3))
                        pe_seq(pe, it * 2 + slot, slot, P, NCMP)
                pe.wait_ge(packs, DB + 3)
                pe_seq(pe, DB, 0, SEQ // CMP_S, NCMP_P)

            @block.scalar
            def _(act):
                act.sem_inc(copied[0], 2)
                act.sem_inc(stored[0], 16)
                act.sem_inc(stored[1], 16)
                with act.Fori(0, DB) as n:
                    act_seq(act, n, P, NCMP)
                act_seq(act, DB, SEQ // CMP_S, NCMP_P)
                for s in range(2):
                    act.wait_ge(stored[s], 16 * (seqs + 1))

            @block.vector
            def _(dve):
                dve.sem_inc(copied[1], 2)
                dve.sem_inc(acted, 2)
                dve.sem_inc(outs_copied, 2)
                with dve.Fori(0, DB) as n:
                    dve_seq(dve, n, P, NCMP)
                dve_seq(dve, DB, SEQ // CMP_S, NCMP_P)


def ssd(nc, ins, outs, proj, y_b, ident):
    NH2 = SH // SG
    CH = PT
    IDX = dict(dA=0, nac=8, eac=16, dt=24, wend=32, dec=40)
    NSM = 44
    with Stage(nc, "ssd") as st:
        x4 = st.sb("x4", [P, 2, SCONV, SCD])
        z = st.sb("z", [P, 2, SIN])
        cw = st.sb("cw", [P, SCONV, SCD])
        cb = st.sb("cb", [P, SCD])
        vec = st.sb("vec", [P, 3, SH])
        gn = st.sb("gn", [P, SIN])
        tri = st.sb("tri", [P, P])
        neg = st.sb("neg", [P, P])
        ones = st.sb("ones", [P, P])
        tri_s = st.sb("tri_s", [NS, NS])
        neg_s = st.sb("neg_s", [NS, NS])
        own_s = st.sb("own_s", [NS, NS])
        row_s = st.sb("row_s", [NS, DB, P])
        col_s = st.sb("col_s", [P, DB, NS])
        small = st.sb("small", [P, CH + 1, NSM])
        tmp = st.sb("tmp", [P, 3, (CH + 1) * SH])
        tot_s = st.sb("tot_s", [P, DB, SH])
        dec_s = st.sb("dec_s", [P, DB, NH2])
        cur = st.sb("cur", [P, 2, NSM])
        sg = st.sb("sg", [P, SCD])
        sz = st.sb("sz", [P, SIN])
        xs = st.sb("xs", [P, SIN])
        xdt = st.sb("xdt", [P, SIN])
        xw = st.sb("xw", [P, SIN])
        bc = st.sb("bc", [P, 2 * P])
        bcT = st.sb("bcT", [P, 2, P])
        ctm = st.sb("ctm", [P, DB, NS])
        bm = st.sb("bm", [NS, DB, P])
        E = st.sb("E", [P, SH, P])
        skip = st.sb("skip", [P, SIN])
        y = st.sb("y", [P, SIN])
        yout = st.sb("yout", [P, 2, SIN])
        junk = st.sb("junk", [P, SIN])
        ss = st.sb("ss", [P, 4])
        state = st.sb("state", [P, NH2 * SP])
        h_raw = st.sb("h_raw", [P, DB, 2, SG * SN])
        h0 = st.sb("h0", [P, DB, NH2 * SP])
        TS = st.ps("TS", [P, 512])
        R = [st.ps(f"R{i}", [P, NH2, P]) for i in range(2)]
        G = [st.ps(f"G{i}", [P, 512]) for i in range(2)]
        Y = st.ps("Y", [P, 512])
        x_pad = nc.dram_tensor("ssd_x_pad", [DB, SCONV - 1 + DT, SCD], F32).ap()

        const_in, zeroed, pad_made, h_in = st.sem("const_in"), st.sem("zeroed"), st.sem("pad_made"), st.sem("h_in")
        step_a, step_d, step_p = st.sem("step_act"), st.sem("step_dve"), st.sem("step_pe")
        K_IN = 16

        def col(name, c=None):
            lo = IDX[name]
            n = NH2 if name == "dec" else SH
            return small[:, :, lo:lo + n] if c is None else small[:, c, lo:lo + n]

        with nc.Block() as block:
            @block.gpsimd
            def _(pool):
                pool.memset(small[:, :, :], 0.0).then_inc(zeroed, 1)
                pool.memset(x4[0:SCONV - 1, 0, :, :], 0.0).then_inc(zeroed, 1)
                pool.memset(state[:, :], 0.0).then_inc(zeroed, 1)

            @block.sync
            def _(sp):
                xbc = slice(C_XBC, C_XBC + SCD)
                sp.dma_start(x_pad[:, 0:SCONV - 1, :], ins["state_ssd_conv"][0]).then_inc(pad_made, 16)
                sp.dma_start(x_pad[:, SCONV - 1:, :], proj[SEQ:TOK, xbc].rearrange("(b t) c -> b t c", t=DT)).then_inc(pad_made, 16)
                sp.wait_ge(zeroed, 1)
                loads = [
                    (small[:, 0:CH, 0:SH], proj[0:SEQ, C_DT:C_DIL].rearrange("(t p) c -> p t c", p=P)),
                    (small[0:NS, CH, 0:SH], proj[SEQ:TOK, C_DT:C_DIL]),
                    (vec[:, 0, :], ins["ssd_dt_bias"][0].partition_broadcast(P)),
                    (vec[:, 1, :], ins["ssd_a_log"][0].partition_broadcast(P)),
                    (vec[:, 2, :], ins["ssd_d"][0].partition_broadcast(P)),
                    (gn[:, :], ins["ssd_norm_g"][0].partition_broadcast(P)),
                    (cb[:, :], ins["ssd_conv_b"][0].partition_broadcast(P)),
                    (tri[:, :], ins["k_tri"]), (neg[:, :], ins["k_neg"]), (ones[:, :], ins["k_ones"]),
                    (tri_s[:, :], ins["k_tri_s"]), (neg_s[:, :], ins["k_neg_s"]), (own_s[:, :], ins["k_own_s"]),
                    (row_s[:, :, :], ins["k_row_s"]), (col_s[:, :, :], ins["k_col_s"]),
                    (cw[:, :, :], ins["ssd_conv_w"][0].partition_broadcast(P)),
                ]
                assert len(loads) == K_IN
                for dst, src in loads:
                    sp.dma_start(dst, src).then_inc(const_in, 16)
                for b in range(DB):
                    for g in range(SG):
                        sp.dma_start(h_raw[:, b, :, g * SN:(g + 1) * SN],
                                     ins["state_ssm"][0, b, g * NH2:(g + 1) * NH2].rearrange("(q a) p n -> (a p) q n", a=2)).then_inc(h_in, 16)
                sp.wait_ge(h_in, 16 * DB * SG)
                sp.wait_ge(pad_made, 32)

            t3 = [tmp[:, i, :].rearrange("p (c h) -> p c h", h=SH) for i in range(3)]

            def over(ap):
                return ap.unsqueeze(1).broadcast_to([P, CH + 1, SH])

            @block.scalar
            def _(act):
                act.wait_ge(const_in, 16 * K_IN)
                act.activation(vec[:, 1, :], vec[:, 1, :], ACT.Exp).then_inc(step_a, 1)
                act.wait_ge(step_d, 1)
                act.activation(t3[1], t3[0], ACT.Abs).then_inc(step_a, 1)
                act.wait_ge(step_a, 2)
                act.activation(t3[1], t3[1], ACT.Exp, scale=-1.0).then_inc(step_a, 1)
                act.wait_ge(step_d, 2)
                act.activation(t3[1], t3[1], ACT.Ln).then_inc(step_a, 1)
                act.wait_ge(step_d, 10)
                act.activation(col("eac"), col("nac"), ACT.Exp, scale=-1.0).then_inc(step_a, 1)
                act.activation(t3[1], t3[1], ACT.Exp).then_inc(step_a, 1)
                act.activation(t3[0], t3[0], ACT.Exp).then_inc(step_a, 1)
                act.activation(tot_s[:, :, :], tot_s[:, :, :], ACT.Exp).then_inc(step_a, 1)

            @block.vector
            def _(dve):
                def link(k, ins_):
                    ins_.then_inc(step_d, 1)
                    dve.wait_ge(step_d, k)

                dve.wait_ge(const_in, 16 * K_IN)
                link(1, dve.tensor_tensor(t3[0], small[:, :, 0:SH], over(vec[:, 0, :]), ALU.add))
                dve.wait_ge(step_a, 3)
                link(2, dve.tensor_scalar(t3[1], t3[1], 1.0, None, ALU.add))
                dve.wait_ge(step_a, 4)
                link(3, dve.scalar_tensor_tensor(col("dt"), t3[0], 0.0, t3[1], ALU.max, ALU.add))
                link(4, dve.scalar_tensor_tensor(col("dA"), col("dt"), -1.0, over(vec[:, 1, :]), ALU.mult, ALU.mult))
                dve.wait_ge(step_p, 1)
                link(5, dve.memset(t3[1][:, CH, :], 0.0))
                link(6, dve.tensor_scalar(small[:, 0:CH, IDX["nac"]:IDX["nac"] + SH], G[0][:, 0:CH * SH].rearrange("p (c h) -> p c h", h=SH),
                                          -1.0, None, ALU.mult))
                link(7, dve.tensor_scalar(small[0:NS, CH, IDX["nac"]:IDX["nac"] + SH], G[1][0:NS, 0:SH], -1.0, None, ALU.mult))
                link(8, dve.tensor_copy(t3[0][:, 0:CH, :], G[0][:, 64:64 + CH * SH].rearrange("p (c h) -> p c h", h=SH)))
                dve.tensor_copy(tot_s[:, :, :].rearrange("p b h -> p (b h)"), G[1][:, 128:128 + DB * SH])
                dve.tensor_tensor(t3[1][0:NS, CH, :], G[1][0:NS, 64:64 + SH], small[0:NS, CH, IDX["nac"]:IDX["nac"] + SH], ALU.add)
                dve.memset(t3[0][:, CH, :], 0.0)
                link(9, dve.memset(ss[:, :], 0.0))
                link(10, dve.tensor_tensor(t3[1][:, 0:CH, :], t3[0][:, 0:CH, :], small[:, 0:CH, IDX["nac"]:IDX["nac"] + SH], ALU.add))
                dve.wait_ge(step_a, 8)
                dve.tensor_tensor(col("wend"), t3[1], col("dt"), ALU.mult)
                for g in range(SG):
                    r = slice(g * SN, (g + 1) * SN)
                    dve.tensor_copy(small[r, 0:CH, IDX["dec"]:IDX["dec"] + NH2], t3[0][r, 0:CH, g * NH2:(g + 1) * NH2])
                    dve.tensor_copy(dec_s[r, :, :], tot_s[r, :, g * NH2:(g + 1) * NH2]).then_inc(step_d, 1)
                for b in range(DB):
                    dve.wait_ge(step_p, 2 + b)
                    dve.tensor_copy(h0[:, b, :], R[b % 2][:, 0:2, :].rearrange("p a n -> p (a n)")).then_inc(step_d, 1)

            @block.tensor
            def _(pe):
                pe.wait_ge(step_d, 4)
                dA = [small[:, c, 0:SH] for c in range(CH)]
                for c in range(CH):
                    pe.matmul(G[0][:, c * SH:(c + 1) * SH], tri[:, :], dA[c], start=True, stop=True)
                    pe.matmul(G[0][:, 64 + c * SH:64 + (c + 1) * SH], ones[:, :], dA[c], start=True, stop=True)
                sA = small[0:NS, CH, 0:SH]
                pe.matmul(G[1][0:NS, 0:SH], tri_s[:, :], sA, start=True, stop=True)
                pe.matmul(G[1][0:NS, 64:64 + SH], own_s[:, :], sA, start=True, stop=True)
                for b in range(DB):
                    mm = pe.matmul(G[1][:, 128 + b * SH:128 + (b + 1) * SH], row_s[:, b, :], sA, start=True, stop=True)
                mm.then_inc(step_p, 1)
                pe.wait_ge(h_in, 16 * DB * SG)
                for b in range(DB):
                    if b >= 2:
                        pe.wait_ge(step_d, 12 + b - 1)
                    for q in range(2):
                        mm = pe.transpose(R[b % 2][:, q, :], h_raw[:, b, q, :], ident[:, :])
                    mm.then_inc(step_p, 1)

        x_in = [st.sem("x_in0"), st.sem("x_in1")]
        cur_made, conv_d, conv_p = st.sem("cur_made"), st.sem("conv_dve"), st.sem("conv_pool")
        sig_x, sig_bc, sig_z = st.sem("sig_x"), st.sem("sig_bc"), st.sem("sig_z")
        x_made, bc_made, zs_made, skip_made = st.sem("x_made"), st.sem("bc_made"), st.sem("zs_made"), st.sem("skip_made")
        bc_turned, bc_copied, ctm_made = st.sem("bc_turned"), st.sem("bc_copied"), st.sem("ctm_made")
        r_made, seg_made, exp_made, m_made = (st.sem(x) for x in ("r_made", "seg_made", "exp_made", "m_made"))
        yd_made, yo_made, st_made = st.sem("y_diag"), st.sem("y_off"), st.sem("st_made")
        yo_read, y_steps, st_updated = st.sem("yo_read"), st.sem("y_steps"), st.sem("st_updated")
        squared, meaned, rooted, normed = st.sem("squared"), st.sem("meaned"), st.sem("rooted"), st.sem("normed")
        stored = [st.sem("stored0"), st.sem("stored1")]
        aside = st.sem("aside")
        XL = 5

        def v3(ap, h=SH):
            return ap.rearrange("p (h d) -> p h d", h=h)

        def cs(m, slot, name):
            lo = IDX[name]
            return cur[0:m, slot, lo:lo + (NH2 if name == "dec" else SH)]

        def convolve(eng, n, slot, m, c0, c1, sem):
            x = x4[0:m, slot, :, c0:c1]
            eng.wait_ge(x_in[slot], x_count(n, slot))
            stand(eng, aside)
            eng.tensor_tensor(x, x, cw[0:m, :, c0:c1], ALU.mult).then_inc(sem, 1)
            eng.wait_ge(sem, n * 4 + 1)
            stand(eng, aside)
            eng.tensor_tensor(x[:, 0:4:2], x[:, 0:4:2], x[:, 1:4:2], ALU.add).then_inc(sem, 1)
            eng.wait_ge(sem, n * 4 + 2)
            stand(eng, aside)
            eng.tensor_tensor(x[:, 0], x[:, 0], x[:, 2], ALU.add).then_inc(sem, 1)
            eng.wait_ge(sem, n * 4 + 3)
            stand(eng, aside)
            eng.tensor_tensor(x[:, 0], x[:, 0], cb[0:m, c0:c1], ALU.add).then_inc(sem, 1)

        def x_count(n, slot):
            if isinstance(n, int):
                return 16 * XL * (n // 2 + 1)
            return (n - slot) * (8 * XL) + 16 * XL

        def pe_chunk(pe, n, slot, m, sample):
            pe.wait_ge(bc_made, n + 1)
            pe.wait_ge(bc_copied, n + 1)
            pe.wait_ge(st_updated, n + 1)
            stand(pe, aside)
            for i in range(2):
                mm = pe.transpose(TS[:, i * P:i * P + m], bc[0:m, i * P:(i + 1) * P], ident[0:m, 0:m])
            mm.then_inc(bc_turned, 1)
            pe.wait_ge(cur_made, n + 1)
            pe.wait_ge(seg_made, n * 2 + 2)
            t = tri_s if sample else tri
            for h in range(SH):
                mm = pe.matmul(R[h // NH2][0:m, h % NH2, 0:m], cs(m, slot, "dA")[:, h:h + 1].broadcast_to([m, m]), t[:, :],
                               start=True, stop=True)
                if h % NH2 == NH2 - 1:
                    mm.then_inc(r_made, 1)
            pe.wait_ge(bc_copied, n + 2)
            pe.wait_ge(yo_read, n + 1)
            stand(pe, aside)
            for g in range(SG):
                r = slice(g * SN, (g + 1) * SN)
                mm = pe.matmul(G[g][0:m, 0:m], bcT[r, 0, 0:m], bcT[r, 1, 0:m], start=True, stop=True)
            pe.wait_ge(st_updated, n + 1)
            if sample:
                pe.wait_ge(ctm_made, 2)
            else:
                stand(pe, aside)
            for g in range(SG):
                r = slice(g * SN, (g + 1) * SN)
                if sample:
                    for b in range(DB):
                        mm = pe.matmul(G[g][0:m, 256:512], ctm[r, b, :], h0[r, b, :], start=(b == 0), stop=(b == DB - 1))
                else:
                    mm = pe.matmul(G[g][0:m, 256:512], bcT[r, 1, 0:m], state[r, :], start=True, stop=True)
            mm.then_inc(yo_made, 1)
            pe.wait_ge(x_made, n * 3 + 3)
            if not sample:
                for g in range(SG):
                    mm = pe.matmul(TS[g * SN:(g + 1) * SN, 256:512], bc[:, g * SN:(g + 1) * SN],
                                   xw[:, g * NH2 * SP:(g + 1) * NH2 * SP], start=True, stop=True)
                mm.then_inc(st_made, 1)
            pe.wait_ge(m_made, n * 2 + 2)
            pe.wait_ge(y_steps, n * 3 + 1)
            for h in range(SH):
                mm = pe.matmul(Y[0:m, h * SP:(h + 1) * SP], E[0:m, h, 0:m], xdt[0:m, h * SP:(h + 1) * SP], start=True, stop=True)
            mm.then_inc(yd_made, 1)

        def act_chunk(act, n, slot, m, sample):
            act.wait_ge(conv_d, n * 4 + 4)
            act.activation(sg[0:m, 0:SIN], x4[0:m, slot, 0, 0:SIN], ACT.Sigmoid).then_inc(sig_x, 1)
            act.wait_ge(conv_p, n * 4 + 4)
            act.activation(sg[0:m, SIN:SCD], x4[0:m, slot, 0, SIN:SCD], ACT.Sigmoid).then_inc(sig_bc, 1)
            act.activation(sz[0:m, :], z[0:m, slot, :], ACT.Sigmoid).then_inc(sig_z, 1)
            act.wait_ge(bc_turned, n + 1)
            act.copy(bcT[:, :, 0:m], TS[:, 0:2 * P].rearrange("p (i j) -> p i j", i=2)[:, :, 0:m]).then_inc(bc_copied, 1)
            for g in range(SG):
                act.wait_ge(seg_made, n * 2 + (2 + g + 1))
                for h in range(g * NH2, (g + 1) * NH2):
                    act.activation(E[0:m, h, 0:m], E[0:m, h, 0:m], ACT.Exp, bias=cs(m, slot, "nac")[:, h:h + 1]).then_inc(exp_made, 1)
            act.wait_ge(y_steps, n * 3 + 4)
            act.activation(junk[0:m, :], y[0:m, :], ACT.Square, accum_out=ss[0:m, 0:1]).then_inc(squared, 1)
            act.wait_ge(meaned, n + 1)
            act.activation(ss[0:m, 2:3], ss[0:m, 1:2], ACT.Sqrt).then_inc(rooted, 1)

        def pool_chunk(pool, n, slot, m, sample):
            convolve(pool, n, slot, m, SIN, SCD, conv_p)
            pool.wait_ge(sig_bc, n + 1)
            pool.wait_ge(st_made, n + 1)
            stand(pool, aside)
            pool.tensor_tensor(bc[0:m, :], x4[0:m, slot, 0, SIN:SCD], sg[0:m, SIN:SCD], ALU.mult).then_inc(bc_made, 1)
            pool.wait_ge(sig_z, n + 1)
            stand(pool, aside)
            pool.tensor_tensor(z[0:m, slot, :], z[0:m, slot, :], sz[0:m, :], ALU.mult).then_inc(zs_made, 1)
            pool.wait_ge(x_made, n * 3 + 1)
            stand(pool, aside)
            pool.tensor_tensor(v3(skip[0:m, :]), v3(xs[0:m, :]), wide(vec[0:m, 2, :], SP), ALU.mult).then_inc(skip_made, 1)
            if sample:
                pool.wait_ge(bc_copied, n + 2)
                pool.tensor_tensor(ctm[:, :, :], bcT[:, 1, 0:NS].unsqueeze(1).broadcast_to([P, DB, NS]), col_s[:, :, :],
                                   ALU.mult).then_inc(ctm_made, 1)
                pool.tensor_tensor(bm[:, :, :], bc[0:NS, 0:P].unsqueeze(1).broadcast_to([NS, DB, P]), row_s[:, :, :],
                                   ALU.mult).then_inc(ctm_made, 1)

        def dve_chunk(dve, n, slot, m, sample):
            src = small[:, CH, :] if sample else small[:, bass.ds(n, 1), :].rearrange("p o k -> p (o k)")
            dve.tensor_copy(cur[:, slot, :], src).then_inc(cur_made, 1)
            convolve(dve, n, slot, m, 0, SIN, conv_d)
            dve.wait_ge(sig_x, n + 1)
            dve.wait_ge(cur_made, n + 1)
            dve.tensor_tensor(xs[0:m, :], x4[0:m, slot, 0, 0:SIN], sg[0:m, 0:SIN], ALU.mult).then_inc(x_made, 1)
            dve.wait_ge(x_made, n * 3 + 1)
            dve.tensor_tensor(v3(xdt[0:m, :]), v3(xs[0:m, :]), wide(cs(m, slot, "dt"), SP), ALU.mult).then_inc(x_made, 1)
            dve.tensor_tensor(v3(xw[0:m, :]), v3(xs[0:m, :]), wide(cs(m, slot, "wend"), SP), ALU.mult).then_inc(x_made, 1)
            mask = (neg_s if sample else neg)[:, :].unsqueeze(1).broadcast_to([m, NH2, m])
            for g in range(SG):
                dve.wait_ge(r_made, n * 2 + (g + 1))
                dve.tensor_tensor(E[0:m, g * NH2:(g + 1) * NH2, 0:m], R[g][0:m, :, 0:m], mask, ALU.add).then_inc(seg_made, 1)
            for g in range(SG):
                e = E[0:m, g * NH2:(g + 1) * NH2, 0:m]
                dve.wait_ge(exp_made, n * 8 + 4 * (g + 1))
                dve.wait_ge(yo_made, n + 1)
                dve.tensor_tensor(e, e, G[g][0:m, 0:m].unsqueeze(1).broadcast_to([m, NH2, m]), ALU.mult).then_inc(m_made, 1)
            for g in range(SG):
                mm = dve.tensor_tensor(v3(y[0:m, g * NH2 * SP:(g + 1) * NH2 * SP], NH2), v3(G[g][0:m, 256:512], NH2),
                                       wide(cs(m, slot, "eac")[:, g * NH2:(g + 1) * NH2], SP), ALU.mult)
            mm.then_inc(yo_read, 1)
            if not sample:
                dve.wait_ge(st_made, n + 2)
                dve.tensor_tensor(v3(state[:, :], NH2), v3(state[:, :], NH2), wide(cs(P, slot, "dec"), SP), ALU.mult).then_inc(decayed, 1)
                dve.wait_ge(decayed, n + 1)
                dve.tensor_tensor(state[:, :], state[:, :], TS[:, 256:512], ALU.add).then_inc(st_updated, 1)
            dve.wait_ge(yo_read, n + 2)
            dve.wait_ge(yd_made, n + 1)
            dve.tensor_tensor(y[0:m, :], y[0:m, :], Y[0:m, :], ALU.add).then_inc(y_steps, 1)
            dve.wait_ge(y_steps, n * 3 + 2)
            dve.wait_ge(skip_made, n + 1)
            dve.tensor_tensor(y[0:m, :], y[0:m, :], skip[0:m, :], ALU.add).then_inc(y_steps, 1)
            dve.wait_ge(y_steps, n * 3 + 3)
            dve.wait_ge(zs_made, n + 1)
            dve.tensor_tensor(y[0:m, :], y[0:m, :], z[0:m, slot, :], ALU.mult).then_inc(y_steps, 1)
            dve.wait_ge(squared, n + 1)
            dve.tensor_scalar(ss[0:m, 1:2], ss[0:m, 0:1], 1.0 / SIN, EPS, ALU.mult, ALU.add).then_inc(meaned, 1)
            dve.wait_ge(rooted, n + 1)
            dve.reciprocal(ss[0:m, 3:4], ss[0:m, 2:3]).then_inc(inverted, 1)
            dve.wait_ge(inverted, n + 1)
            dve.wait_ge(stored[slot], s_count(n, slot))
            dve.scalar_tensor_tensor(yout[0:m, slot, :], y[0:m, :], ss[0:m, 3:4], gn[0:m, :], ALU.mult, ALU.mult).then_inc(normed, 1)

        def s_count(n, slot):
            return 16 * (n // 2 + 1) if isinstance(n, int) else (n - slot) * 8 + 16

        decayed, inverted = st.sem("decayed"), st.sem("inverted")

        with nc.Block() as block:
            @block.sync
            def _(sp):
                sp.sem_inc(stored[0], 16)
                sp.sem_inc(stored[1], 16)

                def load(n):
                    slot = n % 2
                    for k in range(SCONV):
                        back = SCONV - 1 - k
                        if n == CH:
                            sp.dma_start(x4[0:NS, slot, k, :], x_pad[:, k:k + DT, :]).then_inc(x_in[slot], 16)
                        elif n == 0:
                            sp.dma_start(x4[back:P, 0, k, :], proj[0:P - back, C_XBC:C_XBC + SCD]).then_inc(x_in[0], 16)
                        else:
                            sp.dma_start(x4[:, slot, k, :], proj[n * P - back:(n + 1) * P - back, C_XBC:C_XBC + SCD]).then_inc(x_in[slot], 16)
                    r0, m = TILES[n]
                    sp.dma_start(z[0:m, slot, :], proj[r0:r0 + m, C_Z:C_Z + SIN]).then_inc(x_in[slot], 16)

                def store(n):
                    r0, m = TILES[n]
                    sp.wait_ge(normed, n + 1)
                    sp.dma_start(y_b[r0:r0 + m, :], yout[0:m, n % 2, :]).then_inc(stored[n % 2], 16)

                load(0)
                load(1)
                for n in range(CH + 1):
                    store(n)
                    if n + 2 <= CH:
                        load(n + 2)
                sp.wait_ge(stored[0], 16 * 6)
                sp.wait_ge(stored[1], 16 * 5)

            def chunks(eng, body):
                with eng.Fori(0, CH // 2) as it:
                    for slot in range(2):
                        body(eng, it * 2 + slot, slot, P, False)
                body(eng, CH, 0, NS, True)

            @block.tensor
            def _(pe):
                pe.sem_inc(st_made, 1)
                chunks(pe, pe_chunk)

            @block.scalar
            def _(act):
                act.sem_inc(bc_copied, 1)
                chunks(act, act_chunk)

            @block.gpsimd
            def _(pool):
                chunks(pool, pool_chunk)

            @block.vector
            def _(dve):
                dve.sem_inc(seg_made, 2)
                dve.sem_inc(yo_read, 1)
                dve.sem_inc(st_updated, 1)
                dve.sem_inc(y_steps, 1)
                chunks(dve, dve_chunk)

        new = st.sb("new", [P, 2, NH2 * SP])
        rows = st.sb("rows", [P, 2, 2, SG * SN])
        s_made, s_done, s_turned, s_copied = (st.sem(x) for x in ("s_made", "s_done", "s_turned", "s_copied"))
        s_stored = [st.sem("s_stored0"), st.sem("s_stored1")]
        with nc.Block() as block:
            @block.tensor
            def _(pe):
                for b in range(DB + 1):
                    if b < DB:
                        if b >= 2:
                            pe.wait_ge(s_done, 2 * (b - 1))
                        for g in range(SG):
                            mm = pe.matmul(G[b % 2][g * SN:(g + 1) * SN, 0:256], bm[:, b, g * SN:(g + 1) * SN],
                                           xw[0:NS, g * NH2 * SP:(g + 1) * NH2 * SP], start=True, stop=True)
                        mm.then_inc(s_made, 1)
                        pe.wait_ge(s_done, 2 * b + 2)
                    if b >= 2:
                        pe.wait_ge(s_copied, b - 1)
                    src = new[:, b % 2, :] if b < DB else state[:, :]
                    for q in range(2):
                        mm = pe.transpose(R[b % 2][:, q, :], src[:, q * P:(q + 1) * P], ident[:, :])
                    mm.then_inc(s_turned, 1)

            @block.vector
            def _(dve):
                for b in range(DB):
                    if b >= 2:
                        dve.wait_ge(s_turned, b - 1)
                    dve.tensor_tensor(v3(new[:, b % 2, :], NH2), v3(h0[:, b, :], NH2), wide(dec_s[:, b, :], SP), ALU.mult).then_inc(s_done, 1)
                    dve.wait_ge(s_done, 2 * b + 1)
                    dve.wait_ge(s_made, b + 1)
                    dve.tensor_tensor(new[:, b % 2, :], new[:, b % 2, :], G[b % 2][:, 0:256], ALU.add).then_inc(s_done, 1)

            @block.scalar
            def _(act):
                for b in range(DB + 1):
                    act.wait_ge(s_turned, b + 1)
                    if b >= 2:
                        act.wait_ge(s_stored[b % 2], 32 * (b // 2))
                    act.copy(rows[:, b % 2], R[b % 2][:, 0:2, :]).then_inc(s_copied, 1)

            @block.sync
            def _(sp):
                for b in range(DB + 1):
                    sp.wait_ge(s_copied, b + 1)
                    dst = outs["ssm_sample"][0, b] if b < DB else outs["ssm_prompt"][0, 0]
                    for g in range(SG):
                        sp.dma_start(dst[g * NH2:(g + 1) * NH2].rearrange("(q a) p n -> (a p) q n", a=2),
                                     rows[:, b % 2, :, g * SN:(g + 1) * SN]).then_inc(s_stored[b % 2], 16)
                sp.wait_ge(s_stored[0], 32 * 5)
                sp.wait_ge(s_stored[1], 32 * 4)



def nsa_sample(nc, ins, proj, kc_T, vc, o_cmp, o_sel, o_win, ident):
    R = 2 * KVH * NSA_R * DT
    half = R // KVH
    NW, NP_ = WIN // P, CMP_S
    c_win, c_sel = NCMP, NCMP + DT + WIN
    c_new = c_sel + PAST
    width = c_new + DT
    sel_n, win_n = c_new, c_win
    with Stage(nc, "nsas") as st:
        rows = st.sb("rows", [P, 2, CMP_S, 2 * KVH * DH])
        win = st.sb("win", [P, 2, NW, 2 * KVH * DH])
        q_rows = st.sb("q_rows", [R, 2, P])
        new = st.sb("new", [DT, 2, 4 * P])
        kc = st.sb("kc", [P, 2, P])
        vcs = st.sb("vcs", [P, 2, P])
        pages = st.sb("pages", [1, DB * NPAGES], I32)
        sel_T = st.sb("sel_T", [P, CMP_S, P])
        win_T = st.sb("win_T", [P, NW, P])
        qn = st.sb("qn", [P, R + 2 * DT])
        tab = st.sb("tab", [R, width])
        sc = st.sb("sc", [R, width])
        same = st.sb("same", [R, R])
        forced = st.sb("forced", [R, NSEL])
        imp = st.sb("imp", [R, 4 * NSEL + 5])
        score = st.sb("score", [R, NSEL])
        top8 = st.sb("top8", [R, 2, 8])
        pen = st.sb("pen", [R, NSEL])
        stat = st.sb("stat", [R, 4, 4])
        probs_T = st.sb("probs_T", [P, 24, R])
        out = st.sb("out", [R, 2, 3, P])
        T = [st.ps(f"T{i}", [P, 512]) for i in range(2)]
        S = [st.ps(f"S{i}", [P, 512]) for i in range(2)]
        I = st.ps("I", [R, P])
        O = st.ps("O", [R, 3, P])
        const_in, cleared, aside = st.sem("const_in"), st.sem("cleared"), st.sem("aside")
        kv_in = [st.sem("kv_in0"), st.sem("kv_in1")]
        turned, scores, biased = st.sem("turned"), st.sem("scores"), st.sem("biased")
        copied = [st.sem("copied_act"), st.sem("copied_dve")]
        shifted, exped = st.sem("shifted"), st.sem("exped")
        steps = st.sem("selection_steps")
        p_cmp, imp_made, imp_read, pv, normalised = (st.sem(x) for x in ("p_cmp", "imp_made", "imp_read", "pv", "normalised"))
        stored = [st.sem("stored0"), st.sem("stored1")]
        loads_free = st.sem("loads_free")
        LOADS = NPAGES + 1 + 2 * KVH + 1 + 2
        NG = 10
        per_page = PAGE // CMP_S
        misc = [(0, NCMP, 0), (NCMP, DT, win_n), (NCMP + DT, DT, sel_n)]
        units = [misc, [(0, WIN, c_win + DT)]] + [[(0, 512, c_sel + 512 * i)] for i in range(PAST // 512)]
        adds = sum(len(u) for u in units)
        branch = [(0, NCMP), (c_win, c_sel), (c_sel, width)]

        def group_copies(g, slot):
            b = T[g % 2]
            if g < 4:
                return [(sel_T[:, 4 * g:4 * g + 4, :].rearrange("p l n -> p (l n)"), b[:, :])]
            if g == 4:
                return [(win_T[:, :, :].rearrange("p l n -> p (l n)"), b[:, :])]
            if g == 5:
                return [(qn[:, :], b[:, 0:R + 2 * DT])]
            flat = lambda lo, hi, m: probs_T[0:m, lo:hi, :].rearrange("p t r -> p (t r)")
            if g == 6:
                return [(flat(16, 20, P), b[:, 0:4 * R])]
            if g == 7:
                return [(flat(20, 21, NCMP), b[0:NCMP, 0:R]), (flat(21, 23, DT), b[0:DT, R:3 * R])]
            return [(flat(8 * (g - 8), 8 * (g - 7), P), b[:, :])]

        n_copies = [sum(len(group_copies(g, 0)) for g in range(e, NG, 2)) for e in range(2)]
        before = {g: sum(len(group_copies(x, 0)) for x in range(g % 2, g, 2)) for g in range(NG)}

        def copies_done(eng, n, g):
            eng.wait_ge(copied[g % 2], n * n_copies[g % 2] + (before[g] + len(group_copies(g, 0)) + 2))

        def turn(pe, n, g, parts):
            last = before[g] if g >= 2 else 0
            pe.wait_ge(copied[g % 2], n * n_copies[g % 2] + (last + 2))
            stand(pe, aside)
            for dst, src in parts:
                mm = pe.transpose(dst, src, ident[0:src.shape[0], 0:src.shape[0]])
            mm.then_inc(turned, 1)

        def copy(eng, n, g):
            eng.wait_ge(turned, n * NG + (g + 1))
            for i, (dst, src) in enumerate(group_copies(g, 0)):
                (eng.copy if g % 2 == 0 else eng.tensor_copy)(dst, src).then_inc(copied[g % 2], 1)

        def pe_step(pe, n, slot, first):
            pe.wait_ge(kv_in[slot], first * (16 * LOADS) + 16 * LOADS)
            for g in range(4):
                turn(pe, n, g, [(T[g % 2][:, i * P:(i + 1) * P], rows[:, slot, 4 * g + i, 0:P]) for i in range(4)])
            turn(pe, n, 4, [(T[0][:, i * P:(i + 1) * P], win[:, slot, i, 0:P]) for i in range(4)])
            turn(pe, n, 5, [(T[1][:, 0:R], q_rows[:, slot, :]), (T[1][:, R:R + DT], new[:, slot, 0:P]),
                            (T[1][:, R + DT:R + 2 * DT], new[:, slot, 2 * P:3 * P])])
            q = qn[:, 0:R]
            for u in range(len(units)):
                if u == 0:
                    copies_done(pe, n, 5)
                elif u == 1:
                    copies_done(pe, n, 4)
                elif u in (2, 3):
                    copies_done(pe, n, u)
                done = sum(len(x) for x in units[:u - 1]) if u >= 2 else 0
                pe.wait_ge(biased, n * adds + (done + adds if u >= 2 else adds - (1 if u == 0 else 0)))
                if u == 0:
                    pe.matmul(S[0][0:R, 0:NCMP], q, kc[:, slot, 0:NCMP], start=True, stop=True)
                    pe.matmul(S[0][0:R, NCMP:NCMP + DT], q, qn[:, R + DT:R + 2 * DT], start=True, stop=True)
                    mm = pe.matmul(S[0][0:R, NCMP + DT:NCMP + 2 * DT], q, qn[:, R:R + DT], start=True, stop=True)
                elif u == 1:
                    mm = pe.matmul(S[1][0:R, :], q, win_T[:, :, :].rearrange("p l n -> p (l n)"), start=True, stop=True)
                else:
                    mm = pe.matmul(S[u % 2][0:R, :], q, sel_T[:, 4 * (u - 2):4 * (u - 1), :].rearrange("p l n -> p (l n)"),
                                   start=True, stop=True)
                mm.then_inc(scores, 1)
            pe.wait_ge(p_cmp, n * 2 + 2)
            pe.wait_ge(imp_read, n + 1)
            stand(pe, aside)
            pe.matmul(I[:, 0:NCMP], same[:, :], sc[:, 0:NCMP], start=True, stop=True).then_inc(imp_made, 1)
            pe.wait_ge(exped, n * 3 + 2)
            turn(pe, n, 6, [(T[0][:, i * R:(i + 1) * R], sc[:, c_win + DT + i * P:c_win + DT + (i + 1) * P]) for i in range(4)])
            pe.wait_ge(exped, n * 3 + 3)
            turn(pe, n, 7, [(T[1][0:NCMP, 0:R], sc[:, 0:NCMP]), (T[1][0:DT, R:2 * R], sc[:, win_n:win_n + DT]),
                            (T[1][0:DT, 2 * R:3 * R], sc[:, sel_n:sel_n + DT])])
            for g in (8, 9):
                turn(pe, n, g, [(T[g % 2][:, i * R:(i + 1) * R],
                                 sc[:, c_sel + (8 * (g - 8) + i) * P:c_sel + (8 * (g - 8) + i + 1) * P]) for i in range(8)])
            copies_done(pe, n, 9)
            copies_done(pe, n, 8)
            pe.wait_ge(normalised, n + 1)
            stand(pe, aside)
            pe.matmul(O[:, 0, :], probs_T[0:NCMP, 20, :], vcs[0:NCMP, slot, :], start=True, stop=True)
            for i in range(NW):
                pe.matmul(O[:, 1, :], probs_T[:, 16 + i, :], win[:, slot, i, P:2 * P], start=(i == 0), stop=False)
            pe.matmul(O[:, 1, :], probs_T[0:DT, 21, :], new[:, slot, 3 * P:4 * P], start=False, stop=True)
            for i in range(CMP_S):
                pe.matmul(O[:, 2, :], probs_T[:, i, :], rows[:, slot, i, P:2 * P], start=(i == 0), stop=False)
            pe.matmul(O[:, 2, :], probs_T[0:DT, 22, :], new[:, slot, P:2 * P], start=False, stop=True).then_inc(pv, 1)

        def act_step(act, n, slot, first):
            for g in (0, 2, 4):
                copy(act, n, g)
            for br in range(3):
                lo, hi = branch[br]
                act.wait_ge(shifted, n * 3 + (br + 1))
                stand(act, aside)
                act.activation(sc[:, lo:hi], sc[:, lo:hi], ACT.Exp, bias=stat[:, 1, br:br + 1], scale=DH ** -0.5,
                               accum_out=stat[:, 2, br:br + 1]).then_inc(exped, 1)
            for g in (6, 8):
                copy(act, n, g)

        def dve_step(dve, n, slot, first):
            for g in (1, 3, 5):
                copy(dve, n, g)

            def bias(u):
                dve.wait_ge(scores, n * len(units) + (u + 1))
                for c, m, dst in units[u]:
                    dve.tensor_tensor(sc[:, dst:dst + m], S[u % 2][0:R, c:c + m], tab[:, dst:dst + m], ALU.add).then_inc(biased, 1)

            def shift(br, done):
                lo, hi = branch[br]
                dve.wait_ge(biased, n * adds + (adds + done))
                dve.tensor_reduce(stat[:, 0, br:br + 1], sc[:, lo:hi], AX.X, ALU.max).then_inc(steps, 1)
                dve.wait_ge(steps, n * NSTEP + step(1))
                dve.tensor_scalar(stat[:, 1, br:br + 1], stat[:, 0, br:br + 1], -(DH ** -0.5), None, ALU.mult).then_inc(shifted, 1)

            at = [0]

            def step(k):
                at[0] += k
                return at[0]

            bias(0)
            shift(0, 3)
            bias(1)
            shift(1, 4)
            for u in range(2, len(units)):
                bias(u)
            dve.wait_ge(exped, n * 3 + 1)
            dve.reciprocal(stat[:, 3, 3:4], stat[:, 2, 0:1]).then_inc(p_cmp, 1)
            dve.wait_ge(p_cmp, n * 2 + 1)
            dve.tensor_scalar(sc[:, 0:NCMP], sc[:, 0:NCMP], stat[:, 3, 3:4], None, ALU.mult).then_inc(p_cmp, 1)
            dve.wait_ge(imp_made, n + 1)
            dve.tensor_copy(imp[:, 1:1 + NCMP], I[:, 0:NCMP]).then_inc(imp_read, 1)
            dve.wait_ge(imp_read, n + 2)
            ov = [imp[:, o:o + 4 * (NSEL - 1) + 1:4] for o in range(5)]

            def link(i):
                i.then_inc(steps, 1)
                dve.wait_ge(steps, n * NSTEP + step(1))

            link(dve.tensor_tensor(score[:, :], ov[0], ov[1], ALU.add))
            for o in range(2, 5):
                link(dve.tensor_tensor(score[:, :], score[:, :], ov[o], ALU.add))
            link(dve.tensor_tensor(score[:, :], score[:, :], forced[:, :], ALU.add))
            for r in range(SEL_N // 8):
                stand(dve, aside)
                link(dve.max(top8[:, r, :], score[:, :]))
                stand(dve, aside)
                link(dve.match_replace(score[:, :], top8[:, r, :], score[:, :], -3.0e38))
            link(dve.tensor_scalar(pen[:, :], score[:, :], -2.0e38, -BIG, ALU.is_gt, ALU.mult))
            s4 = sc[:, c_sel:c_new].rearrange("r (l j c) -> r l j c", l=CMP_S, c=SEL_L // CMP_S)
            dve.wait_ge(biased, n * adds + 2 * adds)
            last = dve.tensor_tensor(s4, s4, pen[:, 0:PAST // SEL_L].unsqueeze(1).unsqueeze(3).broadcast_to(
                [R, CMP_S, PAST // SEL_L, SEL_L // CMP_S]), ALU.add)
            link(last)
            link(dve.tensor_scalar(sc[:, c_new:width], sc[:, c_new:width], pen[:, NSEL - 1:NSEL], None, ALU.add))
            shift(2, adds)
            for g in (7, 9):
                copy(dve, n, g)
            dve.wait_ge(exped, n * 3 + 3)
            link(dve.reciprocal(stat[:, 3, 1:3], stat[:, 2, 1:3]))
            dve.wait_ge(pv, n + 1)
            dve.wait_ge(stored[slot], first * (16 * 6) + 16 * 6)
            dve.tensor_tensor(out[:, slot], O[:, :, :], wide(stat[:, 3, 0:3], P), ALU.mult).then_inc(normalised, 1)
            assert at[0] == NSTEP, at[0]

        NSTEP = 3 + 4 + 1 + 2 * (SEL_N // 8) + 1 + 2 + 1

        def steps_of(eng, body):
            with eng.Fori(0, DB // 2) as it:
                for slot in range(2):
                    body(eng, it * 2 + slot, slot, it)

        with nc.Block() as block:
            @block.sync
            def _(sp):
                sp.dma_start(pages[:, :], ins["page_table"].rearrange("(o b) n -> o (b n)", o=1)).then_inc(const_in, 16)
                sp.dma_start(tab[:, :], ins["k_nsas_tab"]).then_inc(const_in, 16)
                sp.dma_start(same[:, :], ins["k_nsas_same"]).then_inc(const_in, 16)
                sp.dma_start(forced[:, :], ins["k_nsas_forced"]).then_inc(const_in, 16)
                sp.wait_ge(const_in, 64)
                sp.wait_ge(cleared, 3)
                sel = slice(2 * KVH * DH, 4 * KVH * DH)
                with sp.Fori(0, DB // 2) as it:
                    for slot in range(2):
                        n = it * 2 + slot
                        sp.wait_ge(loads_free, it * 2 + (slot + 1))
                        for j in range(NPAGES):
                            page = sp.value_load(pages[0:1, bass.ds(n * NPAGES + j, 1)], min_val=0,
                                                 max_val=ins["cache_nsa_kv"].shape[1] - 1)
                            src = ins["cache_nsa_kv"][0, bass.ds(page, 1)].rearrange("o (c l) s h d -> (o c) l (s h d)", l=CMP_S)
                            sp.dma_start(rows[j * per_page:(j + 1) * per_page, slot], src[:, :, sel]).then_inc(kv_in[slot], 16)
                        src = ins["cache_nsa_win"][0, bass.ds(n, 1)].rearrange("o (p j) s h d -> (o p) j (s h d)", j=NW)
                        sp.dma_start(win[:, slot], src).then_inc(kv_in[slot], 16)
                        for g in range(KVH):
                            c = C_Q + g * NSA_R * DH
                            src = proj[bass.ds(n * DT + SEQ, DT), c:c + NSA_R * DH].rearrange("t (r d) -> r t d", d=DH)
                            for dup in range(2):
                                r0 = (g * 2 + dup) * NSA_R * DT
                                sp.dma_start(q_rows[r0:r0 + NSA_R * DT, slot, g * DH:(g + 1) * DH], src).then_inc(kv_in[slot], 16)
                        sp.dma_start(new[:, slot, :], proj[bass.ds(n * DT + SEQ, DT), C_KV + 2 * P:C_KV + 6 * P]).then_inc(kv_in[slot], 16)
                        sp.dma_start(kc[:, slot, 0:NCMP], kc_T[bass.ds(n, 1), :, 0:NCMP].rearrange("o p c -> (o p) c")).then_inc(kv_in[slot], 16)
                        sp.dma_start(vcs[0:NCMP, slot, :], vc[bass.ds(n, 1), 0:NCMP, :].rearrange("o p c -> (o p) c")).then_inc(kv_in[slot], 16)

            @block.gpsimd
            def _(pool):
                pool.sem_inc(loads_free, 2)
                pool.memset(q_rows[:, :, :], 0.0).then_inc(cleared, 1)
                pool.memset(imp[:, :], 0.0).then_inc(cleared, 1)
                pool.memset(stat[:, :, :], 1.0).then_inc(cleared, 1)
                with pool.Fori(0, DB) as n:
                    pool.wait_ge(pv, n + 1)
                    pool.sem_inc(loads_free, 1)

            @block.tensor
            def _(pe):
                pe.wait_ge(const_in, 64)
                pe.sem_inc(imp_read, 1)
                steps_of(pe, pe_step)

            @block.scalar
            def _(act):
                act.sem_inc(copied[0], 2)
                act.sem_inc(stored[0], 96)
                act.sem_inc(stored[1], 96)

                def body(eng, n, slot, first):
                    act_step(eng, n, slot, first)
                    eng.wait_ge(normalised, n + 2)
                    for br, o in enumerate((o_cmp, o_win, o_sel)):
                        for g in range(KVH):
                            c = g * NSA_R * DH
                            dst = o[bass.ds(n * DT + SEQ, DT), c:c + NSA_R * DH].rearrange("t (r d) -> r t d", d=DH)
                            eng.dma_start(dst, out[g * half:g * half + NSA_R * DT, slot, br, g * DH:(g + 1) * DH]).then_inc(stored[slot], 16)
                steps_of(act, body)
                for slot in range(2):
                    act.wait_ge(stored[slot], 96 * (DB // 2 + 1))

            @block.vector
            def _(dve):
                dve.wait_ge(const_in, 64)
                dve.wait_ge(cleared, 3)
                dve.sem_inc(copied[1], 2)
                dve.sem_inc(biased, adds)
                dve.sem_inc(normalised, 1)
                steps_of(dve, dve_step)


def batched_rows(nc, name, q_src, loads, seg_of, key_tiles, table, new_kv, store, ins, ident):
    HD = DG * DH
    nseg = sum(len(seg_of(b, kt)) for b in range(DB) for kt in range(key_tiles))
    NK = key_tiles * P + (DT if new_kv else 0)
    by_b = len(seg_of(0, 0)) == 1
    with Stage(nc, name) as st:
        kv = st.sb("kv", [P, nseg, 2 * HD])
        qb = st.sb("qb", [P, NS, HD])
        prod = st.sb("prod", [P, 2, DT, HD])
        s_T = st.sb("s_T", [P, key_tiles, P])
        q_rows = st.sb("q_rows", [P, DH])
        own = st.sb("own", [P, 2, DT, DH])
        own_p = st.sb("own_p", [P, DT, DH])
        tab = st.sb("tab", [P, NK])
        sc = st.sb("sc", [P, NK])
        stat = st.sb("stat", [P, 4])
        p_T = st.sb("p_T", [P, key_tiles, P])
        p_m = st.sb("p_m", [P, nseg, P])
        mask = st.sb("mask", [P, DB if by_b else NS, P])
        diag = st.sb("diag", [P, DG])
        od = st.sb("od", [P, DG, DH])
        acc = st.sb("acc", [P, 2, DH])
        out = st.sb("out", [P, DH])
        T = [st.ps(f"T{i}", [P, key_tiles, P]) for i in range(2)]
        O = st.ps("O", [P, HD])
        small_in, kv_in, q_in = st.sem("small_in"), [st.sem(f"kv_in{b}") for b in range(DB)], st.sem("q_in")
        multiplied, reduced, turned, steps = st.sem("multiplied"), st.sem("reduced"), st.sem("turned"), st.sem("steps")
        exped, masked, pv, stored = st.sem("exped"), st.sem("masked"), st.sem("pv"), st.sem("stored")
        small = [(q_rows[:, :], q_src.rearrange("r (h d) -> r h d", d=DH)), (tab[:, :], table), (diag[:, :], ins["k_diag"]),
                 (mask[:, :, :], ins["k_mask_b" if by_b else "k_mask_bt"])]
        if new_kv:
            for i in range(2):
                s = new_kv[i].rearrange("(b t) (h d) -> b t h d", t=DT, d=DH)
                for b in range(DB):
                    for t in range(DT):
                        r0 = (b * DT + t) * DG
                        small.append((own[r0:r0 + DG, i], s[b].rearrange("t h d -> h t d")))
        pairs = [(b, kt) for kt in range(key_tiles) for b in range(DB)]
        S_MAX = (3 if new_kv else 0) + 3
        S_PT = S_MAX + 1
        S_OUT = S_PT + 1 + 3 + (3 if new_kv else 0)

        with nc.Block() as block:
            @block.sync
            def _(sp):
                sp.dma_start(qb[:, :, :], q_src.partition_broadcast(P)).then_inc(q_in, 16)
                for b in range(DB):
                    dst, src = loads(kv, b)
                    sp.dma_start(dst, src).then_inc(kv_in[b], 16)

            @block.gpsimd
            def _(pool):
                pool.wait_ge(q_in, 16)
                for i, (b, kt) in enumerate(pairs):
                    pool.wait_ge(kv_in[b], 16)
                    if i >= 2:
                        pool.wait_ge(reduced, i - 1)
                    segs = seg_of(b, kt)
                    k = kv[:, segs[0]:segs[-1] + 1, 0:HD]
                    if by_b:
                        k = k.broadcast_to([P, DT, HD])
                    pool.tensor_tensor(prod[:, i % 2], k, qb[:, b * DT:(b + 1) * DT, :], ALU.mult).then_inc(multiplied, 1)
                for kt in range(key_tiles):
                    pool.wait_ge(steps, S_PT)
                    segs = slice(kt * nseg // key_tiles, (kt + 1) * nseg // key_tiles)
                    pool.tensor_tensor(p_m[:, segs, :], mask[:, :, :], p_T[:, kt:kt + 1, :].broadcast_to([P, nseg // key_tiles, P]),
                                       ALU.mult).then_inc(masked, 1)

            @block.tensor
            def _(pe):
                pe.wait_ge(reduced, len(pairs))
                for kt in range(key_tiles):
                    mm = pe.transpose(T[0][:, kt, :], s_T[:, kt, :], ident[:, :])
                mm.then_inc(turned, 1)
                pe.wait_ge(exped, 1)
                for kt in range(key_tiles):
                    mm = pe.transpose(T[1][:, kt, :], sc[:, kt * P:(kt + 1) * P], ident[:, :])
                mm.then_inc(turned, 1)
                pe.wait_ge(masked, key_tiles)
                order = [(kt, b, s) for kt, b in ((kt, b) for kt in range(key_tiles) for b in range(DB)) for s in seg_of(b, kt)]
                for i, (kt, b, s) in enumerate(order):
                    mm = pe.matmul(O[:, :], p_m[:, i, :], kv[:, s, HD:2 * HD], start=(i == 0), stop=(i == nseg - 1))
                mm.then_inc(pv, 1)

            @block.scalar
            def _(act):
                for dst, src in small:
                    act.dma_start(dst, src).then_inc(small_in, 16)
                act.wait_ge(steps, S_MAX)
                act.activation(sc[:, :], sc[:, :], ACT.Exp, bias=stat[:, 1:2], scale=DH ** -0.5, accum_out=stat[:, 2:3]).then_inc(exped, 1)

            @block.vector
            def _(dve):
                at = [0]

                def link(i):
                    at[0] += 1
                    i.then_inc(steps, 1)
                    dve.wait_ge(steps, at[0])

                dve.wait_ge(small_in, 16 * len(small))
                if new_kv:
                    link(dve.tensor_tensor(own_p[:, :, :], own[:, 0], q_rows[:, :].unsqueeze(1).broadcast_to([P, DT, DH]), ALU.mult))
                    link(dve.tensor_reduce(sc[:, key_tiles * P:NK], own_p[:, :, :], AX.X, ALU.add))
                    link(dve.tensor_tensor(sc[:, key_tiles * P:NK], sc[:, key_tiles * P:NK], tab[:, key_tiles * P:NK], ALU.add))
                for i, (b, kt) in enumerate(pairs):
                    dve.wait_ge(multiplied, i + 1)
                    dve.tensor_reduce(s_T[:, kt, b * DT * DG:(b + 1) * DT * DG],
                                      prod[:, i % 2].rearrange("p t (h d) -> p (t h) d", d=DH), AX.X, ALU.add).then_inc(reduced, 1)
                dve.wait_ge(turned, 1)
                link(dve.tensor_tensor(sc[:, 0:key_tiles * P], T[0][:, :, :].rearrange("p k r -> p (k r)"), tab[:, 0:key_tiles * P], ALU.add))
                link(dve.tensor_reduce(stat[:, 0:1], sc[:, :], AX.X, ALU.max))
                link(dve.tensor_scalar(stat[:, 1:2], stat[:, 0:1], -(DH ** -0.5), None, ALU.mult))
                assert at[0] == S_MAX
                dve.wait_ge(turned, 2)
                link(dve.tensor_copy(p_T[:, :, :], T[1][:, :, :]))
                assert at[0] == S_PT
                link(dve.reciprocal(stat[:, 3:4], stat[:, 2:3]))
                if new_kv:
                    link(dve.tensor_tensor(own_p[:, :, :], own[:, 1], wide(sc[:, key_tiles * P:NK], DH), ALU.mult))
                    link(dve.tensor_reduce(acc[:, 1, :], own_p[:, :, :].rearrange("p t d -> p d t"), AX.X, ALU.add))
                dve.wait_ge(pv, 1)
                link(dve.tensor_tensor(od[:, :, :], O[:, :].rearrange("p (h d) -> p h d", d=DH), wide(diag[:, :], DH), ALU.mult))
                link(dve.tensor_reduce(acc[:, 0, :], od[:, :, :].rearrange("p h d -> p d h"), AX.X, ALU.add))
                if new_kv:
                    link(dve.tensor_tensor(acc[:, 0, :], acc[:, 0, :], acc[:, 1, :], ALU.add))
                link(dve.tensor_scalar(out[:, :], acc[:, 0, :], stat[:, 3:4], None, ALU.mult))
                assert at[0] == S_OUT

        with nc.Block() as block:
            @block.sync
            def _(sp):
                moves = store(out, stat)
                for dst, src in moves:
                    sp.dma_start(dst, src).then_inc(stored, 16)
                sp.wait_ge(stored, 16 * len(moves))


def dil_sample(nc, ins, proj, o_dil, ident):
    for g, (w, d) in enumerate(DIL):
        cache = ins[f"cache_dil_w{w}"]
        segs = 1 if d == 1 else DT
        assert w // d == P and (d == 1 or d >= DT)

        def loads(kv, b):
            src = cache[0, b].rearrange("(j r) s h d -> j r (s h d)", r=d)
            return kv[:, b * segs:(b + 1) * segs, :], src[:, 0:segs, :]

        def seg_of(b, kt):
            return list(range(b * segs, (b + 1) * segs))

        c = C_DIL + g * DG * DH
        samples = [proj[SEQ:TOK, c + i * DILH * DH:c + i * DILH * DH + DG * DH] for i in range(3)]

        def store(out, stat):
            o = o_dil[g, SEQ:TOK]
            return [(o[:, :, 0:2 * DH].rearrange("r a (h d) -> r a h d", d=DH), out[:, :]),
                    (o[:, :, 2 * DH:2 * DH + 2].unsqueeze(3), stat[:, 1:2]),
                    (o[:, :, 2 * DH + 2:2 * DH + 4].unsqueeze(3), stat[:, 2:3])]

        batched_rows(nc, f"dils{g}", samples[0], loads, seg_of, 1, ins["k_dils_tab"][g], samples[1:], store, ins, ident)


def combine_branches(nc, proj, o_cmp, o_sel, o_win, o_dil, y_b, ident, o_T):
    n = len(TILES)
    NG = len(DIL)
    with Stage(nc, "comb") as st:
        gates = st.sb("gates", [P, n, 3 * NSA_H])
        stats = st.sb("stats", [P, n, NG, 2, 4])
        lse = st.sb("lse", [P, n, NG, DG])
        top = st.sb("top", [P, n, DG])
        a_in = st.sb("a_in", [P, 2, 3, NSA_H * DH])
        y_in = st.sb("y_in", [P, 2, SIN])
        d_in = st.sb("d_in", [P, 2, NG, 2, 2 * DH])
        ps = [st.ps(f"ps{i}", [P, 4, P]) for i in range(6)]
        small_in = st.sem("small_in")
        cleared = st.sem("cleared")
        tile_in = [st.sem("tile_in0"), st.sem("tile_in1")]
        small, summed_a, summed_c = st.sem("small"), st.sem("summed_a"), st.sem("summed_c")
        turned, copied = st.sem("turned"), st.sem("copied")
        rows_p = "(t p) c -> p t c"
        loads = 7

        with nc.Block() as block:
            @block.sync
            def _(sp):
                sp.wait_ge(cleared, 2)
                sp.dma_start(gates[:, 0:PT, :], proj[0:SEQ, C_GATE:C_Z].rearrange(rows_p, p=P)).then_inc(small_in, 16)
                sp.dma_start(gates[0:NS, PT, :], proj[SEQ:TOK, C_GATE:C_Z]).then_inc(small_in, 16)
                for g in range(NG):
                    for pair in range(2):
                        src = o_dil[g, :, pair, 2 * DH:DCOL]
                        sp.dma_start(stats[:, 0:PT, g, pair, :], src[0:SEQ].rearrange(rows_p, p=P)).then_inc(small_in, 16)
                        sp.dma_start(stats[0:NS, PT, g, pair, :], src[SEQ:TOK]).then_inc(small_in, 16)
                for t, (r0, m) in enumerate(TILES):
                    s = t % 2
                    if t >= 2:
                        sp.wait_ge(turned, 3 * (t - 1))
                    for i, o in enumerate((o_cmp, o_sel, o_win)):
                        sp.dma_start(a_in[0:m, s, i, :], o[r0:r0 + m, :]).then_inc(tile_in[s], 16)
                    sp.dma_start(y_in[0:m, s, :], y_b[r0:r0 + m, :]).then_inc(tile_in[s], 16)
                    for g in range(NG):
                        sp.dma_start(d_in[0:m, s, g], o_dil[g, r0:r0 + m, :, 0:2 * DH]).then_inc(tile_in[s], 16)

            @block.scalar
            def _(act):
                act.wait_ge(small_in, 16 * (2 + 4 * NG))
                act.activation(gates[:, :, :], gates[:, :, :], ACT.Sigmoid).then_inc(small, 1)
                act.activation(lse[:, :, :, :].rearrange("p t g (a h) -> p (t g a) h", a=2),
                               stats[:, :, :, :, 2:4].rearrange("p t g a h -> p (t g a) h"), ACT.Ln).then_inc(small, 1)
                act.wait_ge(small, 5)
                act.activation(lse[:, :, :, :], lse[:, :, :, :], ACT.Exp).then_inc(small, 1)
                for t, (r0, m) in enumerate(TILES):
                    for j in range(3):
                        k = min(4, OK - 4 * j)
                        act.wait_ge(turned, 3 * t + j + 1)
                        act.copy(o_T[:, 4 * j:4 * j + k, r0:r0 + m], ps[(3 * t + j) % 6][:, 0:k, 0:m]).then_inc(copied, 1)

            @block.vector
            def _(dve):
                dve.wait_ge(small, 2)
                dve.tensor_tensor(lse[:, :, :, :].rearrange("p t g (a h) -> p (t g a) h", a=2),
                                  lse[:, :, :, :].rearrange("p t g (a h) -> p (t g a) h", a=2),
                                  stats[:, :, :, :, 0:2].rearrange("p t g a h -> p (t g a) h"), ALU.subtract).then_inc(small, 1)
                dve.wait_ge(small, 3)
                over_g = lse[:, :, :, :].rearrange("p t g h -> p t h g")
                dve.tensor_reduce(top[:, :, :], over_g, AX.X, ALU.max).then_inc(small, 1)
                dve.wait_ge(small, 4)
                dve.tensor_tensor(over_g, over_g, top[:, :, :].unsqueeze(3).broadcast_to([P, n, DG, NG]),
                                  ALU.subtract).then_inc(small, 1)
                dve.wait_ge(small, 6)
                dve.tensor_reduce(top[:, :, :], over_g, AX.X, ALU.add).then_inc(small, 1)
                dve.wait_ge(small, 7)
                dve.reciprocal(top[:, :, :], top[:, :, :]).then_inc(small, 1)
                dve.wait_ge(small, 8)
                dve.tensor_tensor(over_g, over_g, top[:, :, :].unsqueeze(3).broadcast_to([P, n, DG, NG]),
                                  ALU.mult).then_inc(small, 1)
                for t, (r0, m) in enumerate(TILES):
                    s = t % 2
                    dve.wait_ge(tile_in[s], 16 * loads * (t // 2 + 1))
                    a = [a_in[0:m, s, i, :].rearrange("p (h d) -> p h d", d=DH) for i in range(3)]
                    for i in range(3):
                        dve.tensor_tensor(a[i], a[i], wide(gates[0:m, t, i:3 * NSA_H:3], DH), ALU.mult).then_inc(summed_a, 1)
                    dve.wait_ge(summed_a, 5 * t + 2)
                    dve.tensor_tensor(a[0], a[0], a[1], ALU.add).then_inc(summed_a, 1)
                    dve.wait_ge(summed_a, 5 * t + 4)
                    dve.tensor_tensor(a[0], a[0], a[2], ALU.add).then_inc(summed_a, 1)

            @block.gpsimd
            def _(pool):
                pool.memset(gates[:, PT, :], 0.0).then_inc(cleared, 1)
                pool.memset(stats[:, PT], 1.0).then_inc(cleared, 1)
                pool.wait_ge(small, 9)
                for t, (r0, m) in enumerate(TILES):
                    s = t % 2
                    pool.wait_ge(tile_in[s], 16 * loads * (t // 2 + 1))
                    c = [d_in[0:m, s, g].rearrange("p a (h d) -> p (a h) d", d=DH) for g in range(NG)]
                    for g in range(NG):
                        pool.tensor_tensor(c[g], c[g], wide(lse[0:m, t, g, :], DH), ALU.mult).then_inc(summed_c, 1)
                    pool.wait_ge(summed_c, 5 * t + 2)
                    pool.tensor_tensor(c[0], c[0], c[1], ALU.add).then_inc(summed_c, 1)
                    pool.wait_ge(summed_c, 5 * t + 4)
                    pool.tensor_tensor(c[0], c[0], c[2], ALU.add).then_inc(summed_c, 1)

            @block.tensor
            def _(pe):
                for t, (r0, m) in enumerate(TILES):
                    s = t % 2
                    blocks = ([a_in[0:m, s, 0, k * P:(k + 1) * P] for k in range(4)],
                              [y_in[0:m, s, k * P:(k + 1) * P] for k in range(4)],
                              [d_in[0:m, s, 0, k, :] for k in range(2)])
                    for j in range(3):
                        if j == 0:
                            pe.wait_ge(summed_a, 5 * (t + 1))
                        elif j == 1:
                            pe.wait_ge(tile_in[s], 16 * loads * (t // 2 + 1))
                        else:
                            pe.wait_ge(summed_c, 5 * (t + 1))
                        u = 3 * t + j
                        if u >= 6:
                            pe.wait_ge(copied, u - 5)
                        for i, b in enumerate(blocks[j]):
                            mm = pe.transpose(ps[u % 6][:, i, 0:m], b, ident[0:m, 0:m])
                        mm.then_inc(turned, 1)


def merge_branches(nc, ins, u_T, o_T, mix_T):
    chunk = TOK // 3
    with Stage(nc, "mix") as st:
        wg = st.sb("wg", [P, 2, DK, 3, P])
        wb = st.sb("wb", [P, 2, OK, P])
        gate = st.sb("gate", [P, 3, chunk])
        G = [st.ps(f"G{i}", [P, 512]) for i in range(3)]
        B = [st.ps(f"B{i}", [P, 512]) for i in range(3)]
        w_in_sem = [st.sem("w_in0"), st.sem("w_in1")]
        gate_made, branch_made, gated = st.sem("gate_made"), st.sem("branch_made"), st.sem("gated")
        product, merged = st.sem("product"), st.sem("merged")
        ranges = ((0, 4), (4, 8), (8, OK))
        w_gate = ins["w_in"][0, :, C_MG:COLS].rearrange("(k p) (b n) -> p k b n", p=P, b=3)
        branches = [ins[f"w_br_{x}"][0].rearrange("(k p) n -> p k n", p=P) for x in "abc"]
        per_m, dmas = 9, 6

        def load(sp, m, slot):
            for b in range(3):
                sp.dma_start(wg[:, slot, :, b, :], w_gate[:, :, b, bass.ds(m * P, P)]).then_inc(w_in_sem[slot], 16)
                lo, hi = ranges[b]
                sp.dma_start(wb[:, slot, lo:hi, :], branches[b][:, :, bass.ds(m * P, P)]).then_inc(w_in_sem[slot], 16)

        with nc.Block() as block:
            @block.sync
            def _(sp):
                for slot in range(2):
                    load(sp, slot, slot)
                with sp.Fori(0, DK // 2 - 1) as it:
                    for slot in range(2):
                        sp.wait_ge(branch_made, it * (2 * per_m) + per_m * (slot + 1))
                        load(sp, it * 2 + 2 + slot, slot)

            @block.tensor
            def _(pe):
                with pe.Fori(0, DK // 2) as it:
                    for slot in range(2):
                        pe.wait_ge(w_in_sem[slot], it * (16 * dmas) + 16 * dmas)
                        for c in range(3):
                            for b in range(3):
                                u = slot * per_m + c * 3 + b
                                pe.wait_ge(merged, it * (2 * per_m) + (u + 1))
                                for k in range(DK):
                                    mm = pe.matmul(G[b][:, 0:chunk], wg[:, slot, k, b, :], u_T[:, k, c * chunk:(c + 1) * chunk],
                                                   start=(k == 0), stop=(k == DK - 1))
                                mm.then_inc(gate_made, 1)
                                lo, hi = ranges[b]
                                for k in range(lo, hi):
                                    mm = pe.matmul(B[b][:, 0:chunk], wb[:, slot, k, :], o_T[:, k, c * chunk:(c + 1) * chunk],
                                                   start=(k == lo), stop=(k == hi - 1))
                                mm.then_inc(branch_made, 1)

            @block.scalar
            def _(act):
                with act.Fori(0, DK // 2) as it:
                    for u in range(2 * per_m):
                        act.wait_ge(gate_made, it * (2 * per_m) + (u + 1))
                        act.wait_ge(merged, it * (2 * per_m) + (u + 1))
                        act.activation(gate[:, u % 3, :], G[u % 3][:, 0:chunk], ACT.Sigmoid).then_inc(gated, 1)

            @block.vector
            def _(dve):
                dve.sem_inc(merged, 3)
                with dve.Fori(0, DK // 2) as it:
                    for u in range(2 * per_m):
                        c, b = u % per_m // 3, u % 3
                        m = it * 2 + u // per_m
                        out = mix_T[:, bass.ds(m, 1), c * chunk:(c + 1) * chunk].rearrange("p o n -> p (o n)")
                        dve.wait_ge(gated, it * (2 * per_m) + (u + 1))
                        dve.wait_ge(branch_made, it * (2 * per_m) + (u + 1))
                        if b == 0:
                            dve.tensor_tensor(out, gate[:, b, :], B[b][:, 0:chunk], ALU.mult).then_inc(merged, 1)
                        else:
                            dve.tensor_tensor(gate[:, b, :], gate[:, b, :], B[b][:, 0:chunk], ALU.mult).then_inc(product, 1)
                            dve.wait_ge(product, it * 12 + ((u // 3) * 2 + b))
                            dve.wait_ge(merged, it * (2 * per_m) + (u + 3))
                            dve.tensor_tensor(out, out, gate[:, b, :], ALU.add).then_inc(merged, 1)


def project_out(nc, name, lhs_T, blocks, weight, gain_row, x_rows, out_rows):
    ring = 4
    with Stage(nc, name) as st:
        w = st.sb("w", [P, blocks, D])
        gain = st.sb("gain", [P, D])
        xt = st.sb("x", [P, 2, D])
        y = st.sb("y", [P, 2, D])
        ss = st.sb("ss", [P, 4, ring])
        ps = [st.ps(f"ps{i}", [P, D]) for i in range(ring)]
        gain_in, x_in = st.sem("gain_in"), [st.sem("x_in0"), st.sem("x_in1")]
        parts = min(blocks, 4)
        cuts = [blocks * i // parts for i in range(parts + 1)]
        w_in_sem = [st.sem(f"w_in{i}") for i in range(parts)]
        product, squared, meaned, rooted = st.sem("product"), st.sem("squared"), st.sem("meaned"), st.sem("rooted")
        scaled, added = st.sem("scaled"), st.sem("added")
        stored = [st.sem("stored0"), st.sem("stored1")]
        w_k = weight.rearrange("(k p) n -> p k n", p=P)
        n = len(TILES)

        def store(sp, t):
            sp.wait_ge(added, t + 1)
            sp.dma_start(out_rows(t), y[0:TILES[t][1], t % 2, :]).then_inc(stored[t % 2], 16)

        with nc.Block() as block:
            @block.sync
            def _(sp):
                for i in range(parts):
                    sp.dma_start(w[:, cuts[i]:cuts[i + 1], :], w_k[:, cuts[i]:cuts[i + 1], :]).then_inc(w_in_sem[i], 16)
                sp.dma_start(gain[:, :], gain_row.partition_broadcast(P)).then_inc(gain_in, 16)
                for t, (r0, m) in enumerate(TILES):
                    if t >= 2:
                        sp.wait_ge(added, t - 1)
                    sp.dma_start(xt[0:m, t % 2, :], x_rows(t)).then_inc(x_in[t % 2], 16)
                    if t >= 1:
                        store(sp, t - 1)
                store(sp, n - 1)
                for s in range(2):
                    sp.wait_ge(stored[s], 16 * len(range(s, n, 2)))

            @block.tensor
            def _(pe):
                for t, (r0, m) in enumerate(TILES):
                    if t >= ring:
                        pe.wait_ge(scaled, 2 * (t - ring + 1))
                    for i in range(parts):
                        if t == 0:
                            pe.wait_ge(w_in_sem[i], 16)
                        for k in range(cuts[i], cuts[i + 1]):
                            for h in range(2):
                                mm = pe.matmul(ps[t % ring][0:m, 512 * h:512 * (h + 1)], lhs_T[:, k, r0:r0 + m],
                                               w[:, k, 512 * h:512 * (h + 1)], start=(k == 0), stop=(k == blocks - 1))
                    mm.then_inc(product, 1)

            @block.scalar
            def _(act):
                for t, (r0, m) in enumerate(TILES):
                    act.wait_ge(product, t + 1)
                    if t >= 2:
                        act.wait_ge(stored[t % 2], 16 * (t // 2))
                    act.activation(y[0:m, t % 2, :], ps[t % ring][0:m, :], ACT.Square,
                                   accum_out=ss[0:m, 0, t % ring:t % ring + 1]).then_inc(squared, 1)
                    act.wait_ge(meaned, t + 1)
                    act.activation(ss[0:m, 2, t % ring:t % ring + 1], ss[0:m, 1, t % ring:t % ring + 1],
                                   ACT.Sqrt).then_inc(rooted, 1)

            @block.vector
            def _(dve):
                dve.wait_ge(gain_in, 16)
                for t, (r0, m) in enumerate(TILES):
                    s = slice(t % ring, t % ring + 1)
                    dve.wait_ge(squared, t + 1)
                    dve.tensor_scalar(ss[0:m, 1, s], ss[0:m, 0, s], 1.0 / D, EPS, ALU.mult, ALU.add).then_inc(meaned, 1)
                    dve.wait_ge(rooted, t + 1)
                    dve.reciprocal(ss[0:m, 3, s], ss[0:m, 2, s]).then_inc(scaled, 1)
                    dve.wait_ge(scaled, 2 * t + 1)
                    dve.scalar_tensor_tensor(y[0:m, t % 2, :], ps[t % ring][0:m, :], ss[0:m, 3, s], gain[0:m, :],
                                             ALU.mult, ALU.mult).then_inc(scaled, 1)

            @block.gpsimd
            def _(pool):
                for t, (r0, m) in enumerate(TILES):
                    pool.wait_ge(scaled, 2 * t + 2)
                    pool.wait_ge(x_in[t % 2], 16 * (t // 2 + 1))
                    pool.tensor_tensor(y[0:m, t % 2, :], y[0:m, t % 2, :], xt[0:m, t % 2, :], ALU.add).then_inc(added, 1)


def ffn_up(nc, ins, outs, u_T, g_T, ident):
    chunk = TOK // 3
    K = 3
    pad = K - 1
    seg = DT + pad
    s0 = pad + SEQ
    width = s0 + DB * seg
    conv = width - pad
    tail = pad + DB * pad
    NB = DFF // P
    copies = (1, 2, 4, 5, 6, 8)
    with Stage(nc, "ffn") as st:
        w = st.sb("w", [P, 2, DK, 2, P])
        h = st.sb("h", [P, 2, 2, width])
        c = st.sb("c", [P, 2, width])
        sig = st.sb("sig", [P, width])
        tap_raw = st.sb("tap_raw", [2 * NB, K + 1, P])
        taps = st.sb("taps", [P, K + 1, 2 * NB])
        now = st.sb("now", [P, K + 1, 2])
        state = st.sb("state", [DB * pad, 2, 2, P])
        last = st.sb("last", [P, 2, NB, tail])
        last_rows = st.sb("last_rows", [tail, 2 * NB * P])
        ps = [st.ps(f"ps{i}", [P, 512]) for i in range(6)]
        st_ps = st.ps("st_ps", [P, 2, DB * pad])
        tap_in, tap_turned, ready = st.sem("tap_in"), st.sem("tap_turned"), st.sem("ready")
        w_in_sem = [st.sem("w_in0"), st.sem("w_in1")]
        product, st_turned = st.sem("product"), st.sem("state_turned")
        h_copied, st_copied = st.sem("h_copied"), st.sem("state_copied")
        now_copied, convolved, gated = st.sem("now_copied"), st.sem("convolved"), st.sem("gated")
        silu, multiplied, aside = st.sem("silu"), st.sem("multiplied"), st.sem("aside")
        last_packed, last_turned, last_copied = st.sem("last_packed"), st.sem("last_turned"), st.sem("last_copied")
        stored = st.sem("stored")
        w_up = ins["ffn_w_up"][0].rearrange("(k p) (a n) -> p k a n", p=P, a=2)
        state_d = ins["state_ffn_conv"][0].rearrange("b r (a n) -> (b r) a n", a=2)

        def load(q, m, slot):
            for a in range(2):
                q.dma_start(w[:, slot, :, a, :], w_up[:, :, a, bass.ds(m * P, P)]).then_inc(w_in_sem[slot], 16)
            q.dma_start(state[:, slot], state_d[:, :, bass.ds(m * P, P)]).then_inc(w_in_sem[slot], 16)

        def segments(row):
            return row[:, s0:width].rearrange("p (b r) -> p b r", r=seg)

        with nc.Block() as block:
            @block.sync
            def _(sp):
                for k in range(K):
                    sp.dma_start(tap_raw[:, k, :], ins["ffn_conv_w"][0, k].rearrange("(b p) -> b p", p=P)).then_inc(tap_in, 16)
                sp.dma_start(tap_raw[:, K, :], ins["ffn_conv_b"][0].rearrange("(b p) -> b p", p=P)).then_inc(tap_in, 16)
                for slot in range(2):
                    load(sp, slot, slot)
                with sp.Fori(0, NB // 2 - 1) as it:
                    for slot in range(2):
                        sp.wait_ge(product, it * 12 + 6 * (slot + 1))
                        load(sp, it * 2 + 2 + slot, slot)
                sp.wait_ge(last_copied, NB // 2)
                sp.dma_start(outs["ffn_conv_prompt"][0, 0], last_rows[0:pad, :]).then_inc(stored, 16)
                sp.dma_start(outs["ffn_conv_sample"][0].rearrange("b r n -> (b r) n"), last_rows[pad:tail, :]).then_inc(stored, 16)
                sp.wait_ge(stored, 32)

            @block.tensor
            def _(pe):
                pe.wait_ge(tap_in, 16 * (K + 1))
                for k in range(K + 1):
                    mm = pe.transpose(ps[0][:, k * 2 * NB:(k + 1) * 2 * NB], tap_raw[:, k, :], ident[0:2 * NB, 0:2 * NB])
                mm.then_inc(tap_turned, 1)
                pe.wait_ge(ready, 3)
                with pe.Fori(0, NB // 2) as it:
                    for slot in range(2):
                        pe.wait_ge(w_in_sem[slot], it * 48 + 48)
                        pe.wait_ge(st_copied, it * 2 + (slot + 1))
                        stand(pe, aside)
                        for a in range(2):
                            mm = pe.transpose(st_ps[:, a, :], state[:, slot, a, :], ident[0:DB * pad, 0:DB * pad])
                        mm.then_inc(st_turned, 1)
                        for u in range(6):
                            a, x = divmod(u, 3)
                            pe.wait_ge(h_copied, it * 16 + (8 * slot + copies[u]))
                            for k in range(DK):
                                mm = pe.matmul(ps[u][:, 0:chunk], w[:, slot, k, a, :], u_T[:, k, x * chunk:(x + 1) * chunk],
                                               start=(k == 0), stop=(k == DK - 1))
                            mm.then_inc(product, 1)
                pe.wait_ge(last_packed, 4 + 2 * NB)
                pe.wait_ge(h_copied, 8 + 8 * NB)
                for g in range(NB // 2):
                    if g >= 4:
                        pe.wait_ge(last_copied, g - 3)
                    for i in range(4):
                        a, n = divmod(4 * g + i, NB)
                        mm = pe.transpose(ps[g % 4][0:tail, i * P:(i + 1) * P], last[:, a, n, :], ident[:, :])
                    mm.then_inc(last_turned, 1)

            @block.scalar
            def _(act):
                act.sem_inc(h_copied, 8)
                act.wait_ge(ready, 3)
                with act.Fori(0, NB // 2) as it:
                    for slot in range(2):
                        act.wait_ge(convolved, it * 12 + 6 * (slot + 1))
                        act.wait_ge(last_packed, it * 4 + 2 * (slot + 1))
                        for u in range(6):
                            a, x = divmod(u, 3)
                            lo, hi = x * chunk, min((x + 1) * chunk, SEQ)
                            act.wait_ge(product, it * 12 + (6 * slot + u + 1))
                            act.copy(h[:, slot, a, pad + lo:pad + hi], ps[u][:, 0:hi - lo]).then_inc(h_copied, 1)
                            if hi - lo < chunk:
                                act.copy(segments(h[:, slot, a, :])[:, :, pad:seg],
                                         ps[u][:, hi - lo:chunk].rearrange("p (b t) -> p b t", t=DT)).then_inc(h_copied, 1)
                        act.wait_ge(convolved, it * 12 + (6 * slot + 12 + 3))
                        act.wait_ge(multiplied, it * 4 + 2 * (slot + 1))
                        act.activation(sig[:, 0:conv], c[:, 0, 0:conv], ACT.Sigmoid).then_inc(gated, 1)
                for g in range(NB // 2):
                    act.wait_ge(last_turned, g + 1)
                    act.copy(last_rows[:, g * 4 * P:(g + 1) * 4 * P], ps[g % 4][0:tail, :]).then_inc(last_copied, 1)

            @block.vector
            def _(dve):
                dve.sem_inc(st_copied, 1)
                dve.sem_inc(convolved, 12)
                dve.wait_ge(tap_turned, 1)
                dve.tensor_copy(taps[:, :, :].rearrange("p k n -> p (k n)"), ps[0][:, 0:(K + 1) * 2 * NB]).then_inc(ready, 1)
                dve.wait_ge(ready, 3)
                with dve.Fori(0, NB // 2) as it:
                    for slot in range(2):
                        n = it * 2 + slot
                        for a in range(2):
                            dve.tensor_copy(now[:, :, a:a + 1], taps[:, :, bass.ds(n + a * NB, 1)]).then_inc(now_copied, 1)
                        dve.wait_ge(st_turned, it * 2 + (slot + 1))
                        dve.wait_ge(last_packed, it * 4 + 2 * (slot + 1))
                        dve.tensor_copy(h[:, slot, :, s0:width].rearrange("p a (b r) -> p a b r", r=seg)[:, :, :, 0:pad],
                                        st_ps[:, :, :].rearrange("p a (b r) -> p a b r", r=pad)).then_inc(st_copied, 1)
                        dve.wait_ge(st_copied, it * 2 + (slot + 2))
                        dve.wait_ge(now_copied, it * 4 + 2 * (slot + 1))
                        dve.wait_ge(multiplied, it * 4 + 2 * (slot + 1))
                        for a in range(2):
                            row, out = h[:, slot, a, :], c[:, a, 0:conv]
                            base = 6 * slot + 12 + 3 * a
                            dve.wait_ge(h_copied, it * 16 + (8 * slot + 8 + 4 * (a + 1)))
                            dve.tensor_scalar(out, row[:, 0:conv], now[:, 0, a:a + 1], now[:, K, a:a + 1],
                                              ALU.mult, ALU.add).then_inc(convolved, 1)
                            for k in range(1, K):
                                dve.wait_ge(convolved, it * 12 + (base + k))
                                dve.scalar_tensor_tensor(out, row[:, k:k + conv], now[:, k, a:a + 1], out,
                                                         ALU.mult, ALU.add).then_inc(convolved, 1)
                        dve.wait_ge(gated, it * 2 + (slot + 1))
                        dve.wait_ge(convolved, it * 12 + (6 * slot + 12 + 6))
                        dve.tensor_tensor(sig[:, 0:conv], sig[:, 0:conv], c[:, 0, 0:conv], ALU.mult).then_inc(silu, 1)

            @block.gpsimd
            def _(pool):
                pool.sem_inc(last_packed, 4)
                pool.sem_inc(multiplied, 2)
                for slot in range(2):
                    pool.memset(h[:, slot, :, 0:pad], 0.0).then_inc(ready, 1)
                with pool.Fori(0, NB // 2) as it:
                    for slot in range(2):
                        n = it * 2 + slot
                        pool.wait_ge(h_copied, it * 16 + (8 * slot + 16))
                        stand(pool, aside)
                        out = last[:, :, bass.ds(n, 1), :].rearrange("p a o r -> p a (o r)")
                        pool.tensor_copy(out[:, :, 0:pad], h[:, slot, :, SEQ:SEQ + pad]).then_inc(last_packed, 1)
                        pool.tensor_copy(out[:, :, pad:tail].rearrange("p a (b r) -> p a b r", r=pad),
                                         h[:, slot, :, s0:width].rearrange("p a (b r) -> p a b r", r=seg)[:, :, :, DT:seg]).then_inc(last_packed, 1)
                        pool.wait_ge(silu, it * 2 + (slot + 1))
                        stand(pool, aside)
                        out = g_T[:, bass.ds(n, 1), :].rearrange("p o t -> p (o t)")
                        pool.tensor_tensor(out[:, 0:SEQ], sig[:, 0:SEQ], c[:, 1, 0:SEQ], ALU.mult).then_inc(multiplied, 1)
                        pool.tensor_tensor(out[:, SEQ:TOK].rearrange("p (b t) -> p b t", t=DT), segments(sig)[:, :, 0:DT],
                                           segments(c[:, 1, :])[:, :, 0:DT], ALU.mult).then_inc(multiplied, 1)


def memory_kv(nc, ins, outs, m_T):
    cols = 2 * DG * DH
    with Stage(nc, "mkv") as st:
        w = st.sb("w", [P, DK, cols])
        rows = st.sb("rows", [P, 2, cols])
        ps = [st.ps(f"ps{i}", [P, cols]) for i in range(2)]
        w_in, product, copied, stored = (st.sem(x) for x in ("w_in", "product", "copied", "stored"))
        dst = outs["mem_kv_prompt"][0, 0].rearrange("m s h d -> m (s h d)")
        with nc.Block() as block:
            @block.sync
            def _(sp):
                sp.dma_start(w[:, :, :], ins["w_mkv"][0].rearrange("(k p) n -> p k n", p=P)).then_inc(w_in, 16)
                for t in range(2):
                    sp.wait_ge(copied, t + 1)
                    sp.dma_start(dst[t * P:(t + 1) * P], rows[:, t, :]).then_inc(stored, 16)
                sp.wait_ge(stored, 32)

            @block.tensor
            def _(pe):
                pe.wait_ge(w_in, 16)
                for t in range(2):
                    for k in range(DK):
                        mm = pe.matmul(ps[t][:, :], m_T[:, k, t * P:(t + 1) * P], w[:, k, :], start=(k == 0), stop=(k == DK - 1))
                    mm.then_inc(product, 1)

            @block.vector
            def _(dve):
                for t in range(2):
                    dve.wait_ge(product, t + 1)
                    dve.tensor_copy(rows[:, t, :], ps[t][:, :]).then_inc(copied, 1)


def memory_queries(nc, ins, u_T, q_T, q_s):
    HD = DG * DH
    chunk = TOK // 3
    with Stage(nc, "mq") as st:
        w = st.sb("w", [P, DK, HD])
        rows = st.sb("rows", [NS, HD])
        ps = [st.ps(f"ps{i}", [P, 512]) for i in range(7)]
        w_in, product, copied, stored = (st.sem(x) for x in ("w_in", "product", "copied", "stored"))
        with nc.Block() as block:
            @block.sync
            def _(sp):
                sp.dma_start(w[:, :, :], ins["w_mq"][0].rearrange("(k p) n -> p k n", p=P)).then_inc(w_in, 16)
                sp.wait_ge(copied, 1)
                sp.dma_start(q_s, rows[:, :]).then_inc(stored, 16)
                sp.wait_ge(stored, 16)

            @block.tensor
            def _(pe):
                pe.wait_ge(w_in, 16)
                for k in range(DK):
                    mm = pe.matmul(ps[6][0:NS, 0:HD], u_T[:, k, SEQ:TOK], w[:, k, :], start=(k == 0), stop=(k == DK - 1))
                mm.then_inc(product, 1)
                for u in range(6):
                    c, x = divmod(u, 3)
                    for k in range(DK):
                        mm = pe.matmul(ps[u][:, 0:chunk], w[:, k, c * P:(c + 1) * P], u_T[:, k, x * chunk:(x + 1) * chunk],
                                       start=(k == 0), stop=(k == DK - 1))
                    mm.then_inc(product, 1)

            @block.vector
            def _(dve):
                dve.wait_ge(product, 1)
                dve.tensor_copy(rows[:, :], ps[6][0:NS, 0:HD]).then_inc(copied, 1)
                for u in range(6):
                    c, x = divmod(u, 3)
                    dve.wait_ge(product, u + 2)
                    dve.tensor_copy(q_T[:, c, x * chunk:(x + 1) * chunk], ps[u][:, 0:chunk]).then_inc(copied, 1)


def cross_prompt(nc, ins, mem_kv, q_T, o_mem, ident):
    HD = DG * DH
    MT = MEM // P
    with Stage(nc, "xp") as st:
        kv_raw = st.sb("kv_raw", [P, MT, 2 * HD])
        k_T = st.sb("k_T", [P, 2, MEM])
        zero = st.sb("zero", [P, 2, MEM])
        out = st.sb("out", [P, PT, HD])
        kv_in = st.sem("kv_in")
        preps = [([kv_raw[:, t, pair * P:(pair + 1) * P] for t in range(MT)],
                  k_T[:, pair, :].rearrange("d (t k) -> d t k", k=P), P) for pair in range(2)]
        tasks = []
        for h in range(DG):
            pair, r = h // 2, slice(h % 2 * DH, (h % 2 + 1) * DH)
            for t in range(PT):
                tasks.append(dict(q=q_T[r, pair, t * P:(t + 1) * P], k=k_T[r, pair, :], head=h,
                                  table=lambda s: zero[:, s, :],
                                  v=[kv_raw[:, i, HD + h * DH:HD + (h + 1) * DH] for i in range(MT)],
                                  out=out[:, t, h * DH:(h + 1) * DH]))

        def inputs_in(eng, it):
            if eng is nc.tensor:
                eng.wait_ge(kv_in, 16)

        def programs(sp, sems, info):
            sp.dma_start(kv_raw[:, :, :], mem_kv.rearrange("(t p) c -> p t c", p=P)).then_inc(kv_in, 16)
            sp.wait_ge(sems["normalised"], 2 + info["nt"])
            sp.dma_start(o_mem[0:SEQ].rearrange("(t p) c -> p t c", p=P), out[:, :, :]).then_inc(sems["stored"], 16)
            sp.wait_ge(sems["stored"], 32)

        attention(nc, st, 1, preps, tasks, DG, lambda pool, j, slot: pool.memset(zero[:, slot, :], 0.0),
                  ident, inputs_in, programs, 1)


def cross_sample(nc, ins, q_s, o_mem, ident):
    def loads(kv, b):
        src = ins["cache_mem_kv"][0, b].rearrange("(k j) s h d -> j k (s h d)", j=P)
        return kv[:, 2 * b:2 * b + 2, :], src

    def store(out, stat):
        return [(o_mem[SEQ:TOK].rearrange("r (h d) -> r h d", d=DH), out[:, :])]

    batched_rows(nc, "xs", q_s, loads, lambda b, kt: [2 * b + kt], MEM // P, ins["k_zero"], None, store, ins, ident)


def transposed(nc, name, src, blocks, out_T, ident):
    with Stage(nc, name) as st:
        rows = st.sb("rows", [P, 2, blocks * P])
        ps = [st.ps(f"ps{i}", [P, blocks, P]) for i in range(2)]
        rows_in, turned, copied = [st.sem("rows_in0"), st.sem("rows_in1")], st.sem("turned"), st.sem("copied")
        with nc.Block() as block:
            @block.sync
            def _(sp):
                for t, (r0, m) in enumerate(TILES):
                    if t >= 2:
                        sp.wait_ge(turned, t - 1)
                    sp.dma_start(rows[0:m, t % 2, :], src[r0:r0 + m, :]).then_inc(rows_in[t % 2], 16)

            @block.tensor
            def _(pe):
                for t, (r0, m) in enumerate(TILES):
                    pe.wait_ge(rows_in[t % 2], 16 * (t // 2 + 1))
                    if t >= 2:
                        pe.wait_ge(copied, t - 1)
                    for k in range(blocks):
                        mm = pe.transpose(ps[t % 2][:, k, 0:m], rows[0:m, t % 2, k * P:(k + 1) * P], ident[0:m, 0:m])
                    mm.then_inc(turned, 1)

            @block.vector
            def _(dve):
                for t, (r0, m) in enumerate(TILES):
                    dve.wait_ge(turned, t + 1)
                    dve.tensor_copy(out_T[:, :, r0:r0 + m], ps[t % 2][:, :, 0:m]).then_inc(copied, 1)


OUTS = [
    ("y_prompt", (1, SEQ, D)), ("y_sample", (DB, DT, D)),
    ("nsa_kv_prompt", (1, 1, SEQ, 4, KVH, DH)), ("nsa_kv_sample", (1, DB, DT, 4, KVH, DH)),
    ("nsa_win_prompt", (1, 1, WIN, 2, KVH, DH)), ("nsa_win_sample", (1, DB, WIN, 2, KVH, DH)),
    ("ssm_prompt", (1, 1, SH, SP, SN)), ("ssm_sample", (1, DB, SH, SP, SN)),
    ("ssd_conv_prompt", (1, 1, SCONV - 1, SCD)), ("ssd_conv_sample", (1, DB, SCONV - 1, SCD)),
    ("dil128_prompt", (1, 1, 128, 2, DG, DH)), ("dil128_sample", (1, DB, 128, 2, DG, DH)),
    ("dil512_prompt", (1, 1, 512, 2, DG, DH)), ("dil512_sample", (1, DB, 512, 2, DG, DH)),
    ("dil2048_prompt", (1, 1, 2048, 2, DG, DH)), ("dil2048_sample", (1, DB, 2048, 2, DG, DH)),
    ("mem_kv_prompt", (1, 1, MEM, 2, DG, DH)),
    ("ffn_conv_prompt", (1, 1, 2, 2 * DFF)), ("ffn_conv_sample", (1, DB, 2, 2 * DFF)),
]


def decoder_step(nc, ins, outs):
    nc.disable_value_cache = True

    def scratch(name, shape):
        return nc.dram_tensor(name, shape, F32).ap()

    proj = scratch("proj", [TOK, C_MG])
    kc_T, vc = scratch("kc_T", [DB + 1, P, P]), scratch("vc", [DB + 1, P, P])
    o_cmp, o_sel, o_win = (scratch(n, [TOK, NSA_H * DH]) for n in ("o_cmp", "o_sel", "o_win"))
    y_b = scratch("y_b", [TOK, SIN])
    o_dil = scratch("o_dil", [len(DIL), TOK, 2, DCOL])
    moved = nc.alloc_semaphore("caches_moved")
    const = Stage(nc, "const")
    ident = const.sb("ident", [P, P])
    ident_in = nc.alloc_semaphore("ident_in")
    with nc.Block() as block:
        @block.sync
        def _(sp):
            sp.dma_start(ident[:, :], ins["k_ident"]).then_inc(ident_in, 16)
            sp.wait_ge(ident_in, 16)

    x_p = ins["x_prompt"][0]
    x_s = ins["x_sample"].rearrange("b t d -> (b t) d")

    def x_rows(t):
        r0, m = TILES[t]
        return x_p[r0:r0 + m, :] if t < PT else x_s

    def gain(i):
        return ins["norm_g"][0, i].rearrange("(k p) -> k p", p=P)

    mem_kv = outs["mem_kv_prompt"][0, 0].rearrange("m s h d -> m (s h d)")
    x1, x2 = scratch("x1", [TOK, D]), scratch("x2", [TOK, D])
    o_mem, q_s = scratch("o_mem", [TOK, DG * DH]), scratch("q_s", [NS, DG * DH])

    def rows(a):
        return lambda t: a[TILES[t][0]:TILES[t][0] + TILES[t][1], :]

    def y_rows(t):
        r0, m = TILES[t]
        return outs["y_prompt"][0, r0:r0 + m, :] if t < PT else outs["y_sample"].rearrange("b t d -> (b t) d")

    g_row = ins["norm_g"][0]
    moves = cache_moves(ins, proj, outs)
    with Stage(nc, "memory") as part:
        m_T = part.sb("m_T", [P, DK, MEM])
        norm_transposed(nc, "nm", [(0, P), (P, P)], lambda t: ins["mem_prompt"][0, t * P:(t + 1) * P, :],
                        ins["mem_norm_g"][0].rearrange("(k p) -> k p", p=P), ident, m_T)
        memory_kv(nc, ins, outs, m_T)
    with Stage(nc, "mixer") as part:
        u_T = part.sb("u_T", [P, DK, TOK])
        norm_transposed(nc, "n0", TILES, x_rows, gain(0), ident, u_T)
        project_in(nc, u_T, ins["w_in"][0], proj)
    nsa_compress(nc, ins, proj, kc_T, vc, ident)
    nsa_prompt(nc, ins, proj, kc_T, vc, o_cmp, o_sel, o_win, ident, moves, moved)
    nsa_sample(nc, ins, proj, kc_T, vc, o_cmp, o_sel, o_win, ident)
    dil_prompt(nc, ins, proj, o_dil, ident)
    dil_sample(nc, ins, proj, o_dil, ident)
    ssd(nc, ins, outs, proj, y_b, ident)
    with Stage(nc, "merge") as part:
        mix_T = part.sb("mix_T", [P, DK, TOK])
        with Stage(nc, "gates") as inner:
            u_T = inner.sb("u_T", [P, DK, TOK])
            o_T = inner.sb("o_T", [P, OK, TOK])
            norm_transposed(nc, "n1", TILES, x_rows, gain(0), ident, u_T)
            combine_branches(nc, proj, o_cmp, o_sel, o_win, o_dil, y_b, ident, o_T)
            merge_branches(nc, ins, u_T, o_T, mix_T)
        project_out(nc, "out", mix_T, DK, ins["w_out"][0], g_row[1], x_rows, rows(x1))
    with Stage(nc, "cross") as part:
        q_T = part.sb("q_T", [P, 2, TOK])
        o_T = part.sb("o_T", [P, 2, TOK])
        with Stage(nc, "queries") as inner:
            u_T = inner.sb("u_T", [P, DK, TOK])
            norm_transposed(nc, "n2", TILES, rows(x1), gain(2), ident, u_T)
            memory_queries(nc, ins, u_T, q_T, q_s)
        cross_prompt(nc, ins, mem_kv, q_T, o_mem, ident)
        cross_sample(nc, ins, q_s, o_mem, ident)
        transposed(nc, "mt", o_mem, 2, o_T, ident)
        project_out(nc, "mo", o_T, 2, ins["w_mo"][0], g_row[3], rows(x1), rows(x2))
    with Stage(nc, "feed") as part:
        g_T = part.sb("g_T", [P, FFK, TOK])
        with Stage(nc, "up") as inner:
            u_T = inner.sb("u_T", [P, DK, TOK])
            norm_transposed(nc, "n3", TILES, rows(x2), gain(4), ident, u_T)
            ffn_up(nc, ins, outs, u_T, g_T, ident)
        project_out(nc, "down", g_T, FFK, ins["ffn_w_down"][0], g_row[5], rows(x2), y_rows)
    with nc.Block() as block:
        @block.scalar
        def _(act):
            act.wait_ge(moved, 16 * len(moves))


def constants():
    f = np.float32
    p = np.arange(P)[:, None]

    def banded(dist, most=None):
        return np.where((dist >= 0) & (dist <= (SEQ if most is None else most)), dist, BIG).astype(f)

    causal = banded(p + (PT - 1) * P - np.arange(SEQ)[None])
    window = banded(p + WIN - np.arange(WIN + P)[None], WIN - 1)
    ends = np.arange(NCMP_P) * CMP_S + CMP_L - 1
    cmp = np.concatenate([banded(p + t * P - ends[None]) for t in range(PT)], axis=1)
    none, own = np.full((P, P), BIG), p - np.arange(P)[None]
    dil = []
    for w, d in DIL:
        per, reach = SEQ // d, w // d
        both = banded(p + P - np.arange(2 * P)[None], reach)
        if per >= P:
            first = np.concatenate([none, banded(own, reach)], axis=1)
            starts = [(t % (per // P)) == 0 for t in (0, 1, 2)]
            dil.append([first if s else both for s in starts])
        else:
            inside = banded(np.where(p // per == np.arange(P)[None] // per, own, -1), reach)
            dil.append([np.concatenate([none, inside], axis=1)] * 3)
    s_a = 2.0 ** (-8.0 * np.arange(1, NSA_H + 1) / NSA_H)
    s_c = 2.0 ** (-8.0 * np.arange(1, DILH + 1) / DILH)
    stride = np.repeat([d for _, d in DIL], DG)
    root = DH ** 0.5

    def rows(a):
        return np.tile(np.asarray(a, f)[None], (P, 1))

    j, i = np.arange(P)[:, None], np.arange(P)[None]
    js, is_ = j[:NS], i[:, :NS]
    same = js // DT == is_ // DT
    one = np.arange(DB)[None, :, None]
    g, _, r, t = (a.reshape(-1, 1) for a in np.indices((KVH, 2, NSA_R, DT)))
    copy = _
    l, n = (a.reshape(1, -1) for a in np.indices((CMP_S, P)))
    wj, wp = (a.reshape(1, -1) for a in np.indices((WIN // P, P)))
    tn = t - np.arange(DT)[None]
    far = PAST + SEQ

    def upto(dist, most):
        return np.where((dist >= 0) & (dist <= most), dist, BIG)

    dist = np.concatenate([
        PAST + t - (np.arange(NCMP)[None] * CMP_S + CMP_L - 1), upto(tn, far),
        upto(WIN + t - (wp * (WIN // P) + wj), WIN - 1), PAST + t - (CMP_S * n + l), upto(tn, far)], axis=1)
    nsas_tab = (-root * s_a[g * NSA_R + r] * dist).astype(f)
    same_gt = ((g == g.T) & (t == t.T) & (copy == 0)).astype(f)
    blk = np.arange(NSEL)[None]
    last = (PAST + t) // SEL_L
    assert (blk * SEL_L <= PAST).all()
    forced = FORCE * ((blk == 0) | (blk == last) | (blk == last - 1))
    _, t, h = (a.reshape(-1, 1) for a in np.indices((DB, DT, DG)))
    jj, tt = np.arange(P)[None], np.arange(DT)[None]
    dils = []
    for k, (w, d) in enumerate(DIL):
        old = upto(w + t - jj, w) if d == 1 else d * (P - jj) + 0 * t
        mine = upto(t - tt, far) if d == 1 else np.where(tt == t, 0, BIG)
        dils.append(-root * s_c[k * DG + h] * np.concatenate([old, mine], axis=1))
    row = np.arange(P)
    return {
        "k_nsas_tab": nsas_tab, "k_nsas_same": same_gt, "k_nsas_forced": forced.astype(f),
        "k_dils_tab": np.asarray(dils, f), "k_zero": np.zeros((P, MEM), f),
        "k_pad": np.zeros((P, (PAST - SEQ) // P * 2 * DG * DH), f),
        "k_diag": (row[:, None] % DG == np.arange(DG)[None]).astype(f),
        "k_mask_bt": np.tile((row[None, None] // DG == np.arange(NS)[None, :, None]).astype(f), (P, 1, 1)),
        "k_mask_b": np.tile((row[None, None] // (DG * DT) == np.arange(DB)[None, :, None]).astype(f), (P, 1, 1)),
        "k_tri": (j <= i).astype(f), "k_neg": np.where(j <= i, 0, -BIG).astype(f), "k_ones": np.ones((P, P), f),
        "k_tri_s": (same & (js <= is_)).astype(f), "k_neg_s": np.where(same & (js <= is_), 0, -BIG).astype(f),
        "k_own_s": same.astype(f),
        "k_row_s": np.tile((js[:, :, None] // DT == one).astype(f), (1, 1, P)),
        "k_col_s": np.tile((is_[:, None, :] // DT == one).astype(f), (P, 1, 1)),
        "k_ident": np.eye(P, dtype=f),
        "k_nsa_tab": np.concatenate([causal, window, cmp], axis=1).astype(f),
        "k_nsa_slopes": rows(-root * s_a),
        "k_dil_tab": np.ascontiguousarray(np.asarray(dil, f).transpose(0, 2, 1, 3)),
        "k_dil_slopes": rows(-root * s_c * stride),
    }


def kernel(**inputs):
    import concourse.bacc as _bacc
    from concourse.bass_utils import run_bass_kernel_spmd as _run

    nc = _bacc.Bacc("TRN2", target_bir_lowering=False, num_devices=1)
    arrays, ins, outs = {}, {}, {}
    for name, a in list(inputs.items()) + list(constants().items()):
        a = np.ascontiguousarray(a)
        arrays[name] = a
        ins[name] = nc.dram_tensor(name, a.shape, mybir.dt.from_np(a.dtype), kind="ExternalInput").ap()
    for name, shape in OUTS:
        outs[name] = nc.dram_tensor(f"out_{name}", shape, F32, kind="ExternalOutput").ap()
    decoder_step(nc, ins, outs)
    r = _run(nc, [arrays], core_ids=[0]).results[0]
    return tuple(r[f"out_{name}"] for name, _ in OUTS)
```
